# Optimizing a Trainium2 kernel written in Bass

```python
import jax, jax.numpy as jnp
from jax import lax
import numpy as np

D_MODEL = 2048
BATCH = 1
SEQ = 256
DEPTH = 1

CHUNK = 64
HG_HEADS = 8
HG_DK = 128
HG_DV = 128
HG_WIDTH = HG_HEADS * HG_DV
AT_HEADS = 16
AT_DH = 64
AT_WIDTH = AT_HEADS * AT_DH
LEFT_CHUNKS = 8
BAND = (LEFT_CHUNKS + 1) * CHUNK
REL_CLIP = 256
N_REL = 2 * REL_CLIP + 1
D_FF = 4 * D_MODEL
N_BRANCH = 2
EPS = 1e-6
D_IN = 4 * HG_WIDTH + 3 * AT_WIDTH + N_BRANCH * D_MODEL
SPLIT_POINTS = (HG_WIDTH, 2 * HG_WIDTH, 3 * HG_WIDTH, 4 * HG_WIDTH,
                4 * HG_WIDTH + AT_WIDTH, 4 * HG_WIDTH + 2 * AT_WIDTH, 4 * HG_WIDTH + 3 * AT_WIDTH)


def rms_norm(x, w):
    xf = x.astype(jnp.float32)
    y = xf * lax.rsqrt(jnp.mean(xf * xf, axis=-1, keepdims=True) + EPS)
    return (y * w.astype(jnp.float32)).astype(x.dtype)

def hgrn2_scan(q, k, v, log_g):
    B, H, T, DK = q.shape
    DV = v.shape[-1]
    nc = T // CHUNK

    def to_chunks(a):
        return a.reshape(B, H, nc, CHUNK, a.shape[-1]).transpose(2, 0, 1, 3, 4)

    causal = jnp.tril(jnp.ones((CHUNK, CHUNK), dtype=bool))

    def step(S, inp):
        qc, kc, vc, gc = inp
        b = jnp.cumsum(gc, axis=2)
        o_inter = jnp.einsum('bhtk,bhkv->bhtv', qc * jnp.exp(b), S)
        diff = b[:, :, :, None, :] - b[:, :, None, :, :]
        decay = jnp.exp(jnp.where(causal[:, :, None], diff, -jnp.inf))
        scores = jnp.einsum('bhtk,bhtsk,bhsk->bhts', qc, decay, kc)
        o_intra = jnp.einsum('bhts,bhsv->bhtv', scores, vc)
        b_last = b[:, :, -1:, :]
        S_new = jnp.exp(b_last[:, :, 0, :])[..., None] * S + jnp.einsum(
            'bhsk,bhsv->bhkv', kc * jnp.exp(b_last - b), vc)
        return S_new, o_inter + o_intra

    S0 = jnp.zeros((B, H, DK, DV), jnp.float32)
    _, o = lax.scan(step, S0, (to_chunks(q), to_chunks(k), to_chunks(v), to_chunks(log_g)))
    return o.transpose(1, 2, 0, 3, 4).reshape(B, H, T, DV)

def chunk_band_attention(q, k, v, rel_bias):
    B, H, T, Dh = q.shape
    nc = T // CHUNK
    pad = LEFT_CHUNKS * CHUNK
    kp = jnp.pad(k, ((0, 0), (0, 0), (pad, 0), (0, 0)))
    vp = jnp.pad(v, ((0, 0), (0, 0), (pad, 0), (0, 0)))
    idx = (jnp.arange(nc) * CHUNK)[:, None] + jnp.arange(BAND)[None, :]
    kb = kp[:, :, idx, :]
    vb = vp[:, :, idx, :]
    qc = q.reshape(B, H, nc, CHUNK, Dh)
    valid = idx >= pad
    t = jnp.arange(CHUNK)
    j = jnp.arange(BAND)
    rel = t[:, None] + pad - j[None, :]
    rel_idx = jnp.clip(rel, -REL_CLIP, REL_CLIP) + REL_CLIP
    bias = rel_bias[:, rel_idx].astype(jnp.float32)
    s = jnp.einsum('bhnqd,bhnkd->bhnqk', qc, kb).astype(jnp.float32) * (Dh ** -0.5) + bias[:, None]
    s = jnp.where(valid[:, None, :], s, -jnp.inf)
    p = jax.nn.softmax(s, axis=-1).astype(v.dtype)
    o = jnp.einsum('bhnqk,bhnkd->bhnqd', p, vb)
    return o.reshape(B, H, T, Dh)

def mixer_block(u, w_in, lb, hg_norm_w, rel_bias, w_branch_a, w_branch_b, w_out):
    B, T, _ = u.shape
    z = u @ w_in
    hq, hf, hi, hg, aq, ak, av, gates = jnp.split(z, SPLIT_POINTS, axis=-1)

    def to_heads(a, h):
        return a.reshape(B, T, h, -1).transpose(0, 2, 1, 3)

    f = jax.nn.sigmoid(hf.astype(jnp.float32))
    g = lb + (1.0 - lb) * f
    log_g = jnp.log(g)
    kk = 1.0 - g
    q = jax.nn.silu(hq.astype(jnp.float32)) * (HG_DK ** -0.5)
    o = hgrn2_scan(to_heads(q, HG_HEADS), to_heads(kk, HG_HEADS),
                   to_heads(hi.astype(jnp.float32), HG_HEADS), to_heads(log_g, HG_HEADS))
    o = o.transpose(0, 2, 1, 3)
    o = rms_norm(o, hg_norm_w) * jax.nn.silu(hg.reshape(B, T, HG_HEADS, HG_DV).astype(jnp.float32))
    y_a = o.reshape(B, T, HG_WIDTH).astype(u.dtype)

    ya = chunk_band_attention(to_heads(aq, AT_HEADS), to_heads(ak, AT_HEADS),
                              to_heads(av, AT_HEADS), rel_bias)
    y_b = ya.transpose(0, 2, 1, 3).reshape(B, T, AT_WIDTH)

    gate_a, gate_b = jnp.split(jax.nn.sigmoid(gates), 2, axis=-1)
    merged = gate_a * (y_a @ w_branch_a) + gate_b * (y_b @ w_branch_b)
    return merged @ w_out

def first_inputs(seed: int = 0) -> dict:
    key = jax.random.key(seed)
    ks = jax.random.split(key, 13)
    f32 = jnp.float32
    x = jax.random.normal(ks[0], (BATCH, SEQ, D_MODEL), f32)
    w_in = jax.random.normal(ks[1], (DEPTH, D_MODEL, D_IN), f32) * D_MODEL ** -0.5
    lb_logits = jax.random.normal(ks[2], (DEPTH + 1, HG_WIDTH), f32)
    hg_norm_w = 1.0 + 0.02 * jax.random.normal(ks[3], (DEPTH, HG_DV), f32)
    rel_bias = 0.1 * jax.random.normal(ks[4], (DEPTH, AT_HEADS, N_REL), f32)
    w_branch_a = jax.random.normal(ks[5], (DEPTH, HG_WIDTH, D_MODEL), f32) * HG_WIDTH ** -0.5
    w_branch_b = jax.random.normal(ks[6], (DEPTH, AT_WIDTH, D_MODEL), f32) * AT_WIDTH ** -0.5
    w_out = jax.random.normal(ks[7], (DEPTH, D_MODEL, D_MODEL), f32) * D_MODEL ** -0.5
    norm_mix_w = 1.0 + 0.02 * jax.random.normal(ks[8], (DEPTH, D_MODEL), f32)
    norm_mlp_w = 1.0 + 0.02 * jax.random.normal(ks[9], (DEPTH, D_MODEL), f32)
    w_up = jax.random.normal(ks[10], (DEPTH, D_MODEL, D_FF), f32) * D_MODEL ** -0.5
    w_down = jax.random.normal(ks[11], (DEPTH, D_FF, D_MODEL), f32) * D_FF ** -0.5
    norm_final_w = 1.0 + 0.02 * jax.random.normal(ks[12], (D_MODEL,), f32)
    return {"x": x, "w_in": w_in, "lb_logits": lb_logits, "hg_norm_w": hg_norm_w,
            "rel_bias": rel_bias, "w_branch_a": w_branch_a, "w_branch_b": w_branch_b,
            "w_out": w_out, "norm_mix_w": norm_mix_w, "norm_mlp_w": norm_mlp_w,
            "w_up": w_up, "w_down": w_down, "norm_final_w": norm_final_w}

def first_block(x, w_in, lb_logits, hg_norm_w, rel_bias, w_branch_a, w_branch_b, w_out,
              norm_mix_w, norm_mlp_w, w_up, w_down, norm_final_w):
    lb_all = jnp.cumsum(jax.nn.softmax(lb_logits.astype(jnp.float32), axis=0), axis=0)
    h = x
    for l in range(DEPTH):
        h = h + mixer_block(rms_norm(h, norm_mix_w[l]), w_in[l], lb_all[l], hg_norm_w[l],
                            rel_bias[l], w_branch_a[l], w_branch_b[l], w_out[l])
        u = rms_norm(h, norm_mlp_w[l])
        h = h + jnp.square(jax.nn.relu(u @ w_up[l])) @ w_down[l]
    return rms_norm(h, norm_final_w)


GRID_W = 64
GM_GROUPS = 8
GM_HEAD = 128
GM_WIDTH = GM_GROUPS * GM_HEAD
CHUNK_2 = 128
NA_HEADS = 16
NA_HEAD_DIM = 64
NA_WIDTH = NA_HEADS * NA_HEAD_DIM
NA_KR = 8
NA_KC = 16
IN_COLS = 2 * GM_WIDTH + 3 * NA_WIDTH + N_BRANCH * D_MODEL
D_FF_2 = 5504
CONV_W = 3
RMS_EPS = 1e-6
LN_EPS = 1e-5
NEG_INF = -1e30


def rms_norm_2(x, g):
    xf = x.astype(jnp.float32)
    y = xf * lax.rsqrt(jnp.mean(xf * xf, axis=-1, keepdims=True) + RMS_EPS)
    return (y * g.astype(jnp.float32)).astype(x.dtype)

def gmlp_branch(uv, ln_g, ln_b, w_s, b_s):
    b, t, _ = uv.shape
    uv = jax.nn.gelu(uv)
    u, v = jnp.split(uv, 2, axis=-1)
    vf = v.astype(jnp.float32)
    mu = jnp.mean(vf, axis=-1, keepdims=True)
    var = jnp.mean(jnp.square(vf - mu), axis=-1, keepdims=True)
    v = ((vf - mu) * lax.rsqrt(var + LN_EPS) * ln_g.astype(jnp.float32)
         + ln_b.astype(jnp.float32)).astype(u.dtype)
    v = v.reshape(b, t // CHUNK_2, CHUNK_2, GM_GROUPS, GM_HEAD)
    mixed = jnp.einsum('gpq,bnqgc->bnpgc', w_s, v) + b_s.T[None, None, :, :, None]
    return u * mixed.reshape(b, t, GM_WIDTH)

def neighbourhood_attn(q, k, v, rpb):
    b, t, _ = q.shape
    rows = t // GRID_W
    kr = min(NA_KR, rows)

    def to_grid(z):
        return z.reshape(b, rows, GRID_W, NA_HEADS, NA_HEAD_DIM).transpose(0, 3, 1, 2, 4)

    qg, kg, vg = to_grid(q), to_grid(k), to_grid(v)
    r = jnp.arange(rows)
    row_start = jnp.clip(r - kr // 2, 0, rows - kr)
    row_idx = row_start[:, None] + jnp.arange(kr)[None, :]
    k_blk = kg[:, :, row_idx]
    v_blk = vg[:, :, row_idx]

    c = jnp.arange(GRID_W)
    col_start = jnp.clip(c - NA_KC // 2, 0, GRID_W - NA_KC)
    in_win = (c[None, :] >= col_start[:, None]) & (c[None, :] < col_start[:, None] + NA_KC)
    dr_i = (row_idx - r[:, None]) + (NA_KR - 1)
    dc_i = jnp.clip(c[None, :] - c[:, None], -(NA_KC - 1), NA_KC - 1) + (NA_KC - 1)
    bias = rpb.astype(jnp.float32)[:, dr_i[:, None, :, None], dc_i[None, :, None, :]]
    bias = jnp.where(in_win[None, None, :, None, :], bias, NEG_INF)

    scale = NA_HEAD_DIM ** -0.5
    s = jnp.einsum('bhrcd,bhrikd->bhrcik', qg.astype(jnp.float32),
                   k_blk.astype(jnp.float32)) * scale + bias[None]
    p = jax.nn.softmax(s.reshape(b, NA_HEADS, rows, GRID_W, kr * GRID_W), axis=-1)
    p = p.reshape(b, NA_HEADS, rows, GRID_W, kr, GRID_W)
    o = jnp.einsum('bhrcik,bhrikd->bhrcd', p, v_blk.astype(jnp.float32))
    return o.transpose(0, 2, 3, 1, 4).reshape(b, t, NA_WIDTH).astype(q.dtype)

def mixer_block_2(x, g_norm, w_in, ln_g, ln_b, w_s, b_s, rpb, w_branch, w_out):
    h = rms_norm_2(x, g_norm)
    proj = h @ w_in
    uv, qkv, gates = jnp.split(proj, [2 * GM_WIDTH, 2 * GM_WIDTH + 3 * NA_WIDTH], axis=-1)
    q, k, v = jnp.split(qkv, 3, axis=-1)
    y_a = gmlp_branch(uv, ln_g, ln_b, w_s, b_s)
    y_b = neighbourhood_attn(q, k, v, rpb)
    g_a, g_b = jnp.split(jax.nn.sigmoid(gates), 2, axis=-1)
    merged = g_a * (y_a @ w_branch[:GM_WIDTH]) + g_b * (y_b @ w_branch[GM_WIDTH:])
    return x + merged @ w_out

def conv_ffn(x, g_norm, w_up, conv_k, conv_b, w_down):
    h = rms_norm_2(x, g_norm)
    up = h @ w_up
    t = up.shape[1]
    pad = jnp.pad(up, ((0, 0), (1, 1), (0, 0)))
    up = (pad[:, :t] * conv_k[0] + pad[:, 1:t + 1] * conv_k[1]
          + pad[:, 2:t + 2] * conv_k[2] + conv_b)
    gate, val = jnp.split(up, 2, axis=-1)
    return x + (jax.nn.silu(gate) * val) @ w_down

def second_inputs(seed: int = 0) -> dict:
    key = jax.random.key(seed)
    ks = jax.random.split(key, 17)
    f32 = jnp.float32
    n = lambda k, s: jax.random.normal(k, s, f32)
    return {
        "x": n(ks[0], (BATCH, SEQ, D_MODEL)),
        "norm_mix": 1.0 + 0.1 * n(ks[1], (DEPTH, D_MODEL)),
        "w_in": n(ks[2], (DEPTH, D_MODEL, IN_COLS)) * D_MODEL ** -0.5,
        "gm_ln_g": 1.0 + 0.1 * n(ks[3], (DEPTH, GM_WIDTH)),
        "gm_ln_b": 0.01 * n(ks[4], (DEPTH, GM_WIDTH)),
        "gm_w_s": n(ks[5], (DEPTH, GM_GROUPS, CHUNK_2, CHUNK_2)) * CHUNK_2 ** -0.5,
        "gm_b_s": 1.0 + 0.1 * n(ks[6], (DEPTH, GM_GROUPS, CHUNK_2)),
        "na_rpb": 0.5 * n(ks[7], (DEPTH, NA_HEADS, 2 * NA_KR - 1, 2 * NA_KC - 1)),
        "w_branch": n(ks[8], (DEPTH, GM_WIDTH + NA_WIDTH, D_MODEL)) * GM_WIDTH ** -0.5,
        "w_out": n(ks[9], (DEPTH, D_MODEL, D_MODEL)) * D_MODEL ** -0.5,
        "norm_ffn": 1.0 + 0.1 * n(ks[10], (DEPTH, D_MODEL)),
        "w_up": n(ks[11], (DEPTH, D_MODEL, 2 * D_FF_2)) * D_MODEL ** -0.5,
        "conv_k": n(ks[12], (DEPTH, CONV_W, 2 * D_FF_2)) * CONV_W ** -0.5,
        "conv_b": 0.01 * n(ks[13], (DEPTH, 2 * D_FF_2)),
        "w_down": n(ks[14], (DEPTH, D_FF_2, D_MODEL)) * D_FF_2 ** -0.5,
        "norm_final": 1.0 + 0.1 * n(ks[15], (D_MODEL,)),
    }

def second_block(x, norm_mix, w_in, gm_ln_g, gm_ln_b, gm_w_s, gm_b_s, na_rpb, w_branch, w_out,
              norm_ffn, w_up, conv_k, conv_b, w_down, norm_final):
    for l in range(DEPTH):
        x = mixer_block_2(x, norm_mix[l], w_in[l], gm_ln_g[l], gm_ln_b[l], gm_w_s[l], gm_b_s[l],
                        na_rpb[l], w_branch[l], w_out[l])
        x = conv_ffn(x, norm_ffn[l], w_up[l], conv_k[l], conv_b[l], w_down[l])
    return rms_norm_2(x, norm_final)


def setup_inputs(seed=0):
    out = dict(first_inputs(seed))
    for name, value in second_inputs(seed + 1).items():
        if name != "x":
            out[name + "_2"] = value
    return out


def reference(
    x, w_in, lb_logits, hg_norm_w, rel_bias, w_branch_a, w_branch_b, w_out, norm_mix_w,
    norm_mlp_w, w_up, w_down, norm_final_w, norm_mix_2, w_in_2, gm_ln_g_2, gm_ln_b_2, gm_w_s_2,
    gm_b_s_2, na_rpb_2, w_branch_2, w_out_2, norm_ffn_2, w_up_2, conv_k_2, conv_b_2, w_down_2,
    norm_final_2,
):
    x = first_block(
        x, w_in, lb_logits, hg_norm_w, rel_bias, w_branch_a, w_branch_b, w_out, norm_mix_w,
        norm_mlp_w, w_up, w_down, norm_final_w,
    )
    return second_block(
        x, norm_mix_2, w_in_2, gm_ln_g_2, gm_ln_b_2, gm_w_s_2, gm_b_s_2, na_rpb_2, w_branch_2,
        w_out_2, norm_ffn_2, w_up_2, conv_k_2, conv_b_2, w_down_2, norm_final_2,
    )


_drawn_inputs = setup_inputs


def setup_inputs(seed=0):
    import zlib

    import numpy as np

    out = dict(_drawn_inputs(seed))
    spreads = {}
    factors = {'hg_norm_w': 6.794,
     'rel_bias': 5.947,
     'norm_mix_w': 4.459,
     'gm_ln_b_2': 8.0,
     'conv_b_2': 8.0,
     'norm_mlp_w': 8.0}
    for name, (base, spread) in spreads.items():
        noise = np.random.default_rng([zlib.crc32(name.encode()), seed]).standard_normal(out[name].shape)
        drawn = base * np.exp(spread * noise) if base else spread * noise
        out[name] = __import__('jax').numpy.asarray(drawn.astype(out[name].dtype))
    for name, factor in factors.items():
        out[name] = (out[name] * factor).astype(out[name].dtype)
    return out
```

```python
from contextlib import ExitStack

import concourse.bass as bass
import numpy as np
from concourse import mybir

F32 = mybir.dt.float32
F32R = mybir.dt.float32r
BF16 = mybir.dt.bfloat16
ALU = mybir.AluOpType
ACT = mybir.ActivationFunctionType
AX_X = mybir.AxisListType.X
ds = bass.ds

P = 128
T = 256
NT = T // P
D = 2048
KD = D // P
HEADS = 8
WIDTH = HEADS * P
FF1 = 4 * D // P
FF2 = 5504 // P
N_REL = 513
RPB_R, RPB_C = 15, 31
AT_SCALE = 64 ** -0.5
HG_SCALE = P ** -0.5
MASKED = -3.0e38
RMS_EPS = 1e-6
LN_EPS = 1e-5
NREL_COLS = 384
RPB_BACK = RPB_R * RPB_C - 1 - (10 * RPB_C + 63 + 15)

SLOTS = 5
REUSE = 4
LEAD = 4
KB = 8
BLOCK = KB * P


class Phase:

    def __init__(self, name, before, iters, blocks, tiles, crosses, shapes=None):
        self.name, self.iters, self.blocks, self.tiles, self.crosses = name, iters, blocks, tiles, crosses
        fives = next(n for n in range(blocks) if (blocks - 5 * n) % 4 == 0)
        self.slots = [s for n in [5] * fives + [4] * ((blocks - 5 * fives) // 4) for s in range(n)]
        self.uses = [self.slots.count(s) for s in range(SLOTS)]
        if before is None:
            self.base, self.tbase, self.cbase, self.used = 0, 0, 0, [0] * SLOTS
        else:
            self.base = before.base + before.iters * before.blocks
            self.tbase = before.tbase + before.iters * before.tiles
            self.cbase = before.cbase + before.iters * before.crosses
            self.used = [u + before.iters * n for u, n in zip(before.used, before.uses)]
        self.shapes = shapes or {}

    def block(self, i, b):
        return self.base + self.blocks * i + b

    def tile(self, i, t):
        return self.tbase + self.tiles * i + t

    def cross(self, i, c):
        return self.cbase + self.crosses * i + c

    def slot(self, b):
        return self.slots[b] if b < self.blocks else b - self.blocks

    def landed(self, i, b):
        s = self.slot(b)
        if b < self.blocks:
            return (self.used[s] + self.slots[:b].count(s) + 1) * 16 + self.uses[s] * 16 * i
        return (self.used[s] + self.uses[s] + 1) * 16 + self.uses[s] * 16 * i

    def size(self, b):
        kt, cols = self.shapes.get(b, (KB, P))
        return kt * cols


def phases():
    tail = {b: (FF2 % KB, 2 * P) for b in range(4 * (FF2 % KB), 4 * (FF2 % KB) + KD // 2)}
    plan = [("heads1", HEADS, 22, 11, 11, None), ("branch1", 2, 16, 16, 16, None),
            ("out1", 2, 16, 8, 0, None), ("ffn1", FF1 // KB - 1, 32, 24, 8, None),
            ("ffn1last", 1, 32, 24, 8, None), ("gmv", 1, 16, 8, 8, None),
            ("heads2", HEADS, 16, 8, 8, None), ("branch2", 2, 16, 16, 16, None),
            ("out2", 2, 16, 8, 0, None), ("ffn2tail", 1, 20, 22, 6, tail),
            ("ffn2", FF2 // KB - 1, 48, 32, 16, None), ("ffn2last", 1, 48, 32, 16, None)]
    out, before = {}, None
    for name, iters, blocks, tiles, crosses, shapes in plan:
        before = out[name] = Phase(name, before, iters, blocks, tiles, crosses, shapes)
    return out


class Link:

    def __init__(self, eng, sem):
        self.eng, self.sem, self.base, self.k, self.i, self.per = eng, sem, 0, 0, None, 0

    def __call__(self, ins):
        self.k += 1
        ins.then_inc(self.sem, 1)
        at = self.base + self.k
        self.eng.wait_ge(self.sem, at if self.i is None else self.i * self.per + at)

    def enter(self, i, per):
        self.base, self.k, self.i, self.per = self.base + self.k, 0, i, per

    def leave(self, n):
        assert self.k == self.per, (self.k, self.per)
        self.base, self.k, self.i = self.base + n * self.per, 0, None


def two_blocks(
    nc, x, w_in, lb_logits, hg_norm_w, rel_bias, w_branch_a, w_branch_b, w_out, norm_mix_w, norm_mlp_w,
    w_up, w_down, norm_final_w, norm_mix_2, w_in_2, gm_ln_g_2, gm_ln_b_2, gm_w_s_2, gm_b_s_2, na_rpb_2,
    w_branch_2, w_out_2, norm_ffn_2, w_up_2, conv_k_2, conv_b_2, w_down_2, norm_final_2,
    range_sums, pair_masks, identity, window, out,
):
    ph = phases()
    last_phase = ph["ffn2last"]
    total_blocks = last_phase.base + last_phase.blocks

    with ExitStack() as ctx:
        def sb(name, shape, dt=F32):
            return ctx.enter_context(nc.sbuf_tensor(name, shape, dt))

        def psum(name):
            return ctx.enter_context(nc.psum_tensor(name, [P, 512], F32))

        def sem(name):
            return ctx.enter_context(nc.semaphore(name))

        w_raw = [sb(f"w_raw{s}", [P, BLOCK]) for s in range(SLOTS)]
        w_hi = [sb(f"w_hi{s}", [P, BLOCK], F32R) for s in range(SLOTS)]
        w_lo = [sb(f"w_lo{s}", [P, BLOCK], F32R) for s in range(SLOTS)]
        hT = sb("hT", [P, KD, T])
        XU = sb("XU", [P, KD, 2 * T], F32R)
        XY = sb("XY", [P, KD, 2 * T], F32R)
        G = sb("G", [P, 2 * KD, T])
        Gf = G[:, :, :].rearrange("p a t -> p (a t)")
        sums = sb("sums", [P, 9, P], F32R)
        masks = sb("masks", [P, 9, P], BF16)
        ident = sb("ident", [P, P])
        ones = sb("ones", [P, P])
        cols = sb("cols", [P, P])
        convc = sb("convc", [P, 4, 2 * FF2])
        small = sb("small", [P, 64])
        HS = sb("HS", [P, 4, 4, P])
        work = sb("work", [P, 9, T + 2])
        cross = sb("cross", [P, 2, T])
        rs = sb("rs", [P, T])
        rs1 = sb("rs1", [P, T])
        sqacc = sb("sqacc", [P, 2, T])
        sqb = sb("sqb", [P, 2, T])
        lg_hi = sb("lg_hi", [P, NT, P], F32R)
        lg_lo = sb("lg_lo", [P, NT, P], F32R)
        AT = sb("AT", [P, 3, P])
        kTop = sb("kTop", [P, P])
        v_nat = sb("v_nat", [P, NT, P])
        av_nat = sb("av_nat", [P, NT, P])
        probs = sb("probs", [P, NT, 2, T])
        pT = sb("pT", [P, 4, P])
        bias = sb("bias", [P, 2, NREL_COLS])
        soft = sb("soft", [P, 4, 2, 2])

        acc = [psum("acc0"), psum("acc1")]
        psE, psA, psT, psS, psX = (psum(n) for n in ("psE", "psA", "psT", "psS", "psX"))

        rpb_back = nc.dram_tensor("rpb_back", (2 * HEADS, RPB_R * RPB_C), F32, kind="Internal").ap()

        C_MIX1, C_MLP1, C_FIN1, C_MIX2, C_FFN2, C_FIN2, C_LB, C_LNG, C_LNB = 0, 16, 32, 48, 64, 80, 96, 112, 120
        eps_rms, eps_ln, hgw = small[:, 0:1], small[:, 1:2], small[:, 2:3]
        lbc, omlb, fm2 = small[:, 8:16], small[:, 16:24], small[:, 24:40]
        lbt = small[:, 40:64]

        def wk(n):
            return work[:, n, 0:T]

        landed = [sem(f"landed{s}") for s in range(SLOTS)]
        hi_done, lo_dve, lo_pool, w_used = sem("hi_done"), sem("lo_dve"), sem("lo_pool"), sem("w_used")
        acc_free, cross_ready = sem("acc_free"), sem("cross_ready")
        dve_step, act_step, pool_step = sem("dve_step"), sem("act_step"), sem("pool_step")
        x_in, c_in, v_in = sem("x_in"), sem("c_in"), sem("v_in")
        h_ready, sq_ready, sq_added, uh_ready, x_ready = (
            sem(n) for n in ("h_ready", "sq_ready", "sq_added", "uh_ready", "x_ready"))
        sq2_ready, sq2_added = sem("sq2_ready"), sem("sq2_added")
        stat_done, rs_ready = sem("stat_done"), sem("rs_ready")
        names = {}

        def S(name):
            if name not in names:
                names[name] = sem(name)
            return names[name]

        CREDIT = REUSE
        TILE_CREDIT = 2

        block = ctx.enter_context(nc.Block())

        def weight_source(name, i, b):
            def part(w, row, ntiles, col, ncols=P):
                n = w.shape[1]
                return w.tensor, row * n + col, [[n, P], [P * n, ntiles], [1, ncols]]

            half = b % 2
            if name == "heads1":
                t = b // 2
                starts = [0, 1, 3, 2, 5, 4, 6]
                col = starts[t] * WIDTH + i * P if t < 7 else (7 * WIDTH + (t - 7) // 2 * D + (t - 7) % 2 * P + i * (2 * P))
                return part(w_in[0], half * BLOCK, KB, col)
            if name == "heads2":
                t = b // 2
                starts = [0, 3, 2, 4]
                col = starts[t] * WIDTH + i * P if t < 4 else (5 * WIDTH + (t - 4) // 2 * D + (t - 4) % 2 * P + i * (2 * P))
                return part(w_in_2[0], half * BLOCK, KB, col)
            if name == "gmv":
                return part(w_in_2[0], half * BLOCK, KB, WIDTH + b // 2 * P)
            if name == "branch1":
                return part((w_branch_a, w_branch_b)[half][0], 0, KB, i * (8 * P) + b // 2 * P)
            if name == "branch2":
                return part(w_branch_2[0], half * BLOCK, KB, i * (8 * P) + b // 2 * P)
            if name in ("out1", "out2"):
                return part((w_out if name == "out1" else w_out_2)[0], half * BLOCK, KB, i * (8 * P) + b // 2 * P)
            if name in ("ffn1", "ffn1last"):
                if b < 2 * KB:
                    return part(w_up[0], half * BLOCK, KB, i * BLOCK + b // 2 * P)
                return part(w_down[0], i * BLOCK, KB, (b - 2 * KB) * P)
            first = 0 if name == "ffn2tail" else (FF2 % KB) * P
            nk = FF2 % KB if name == "ffn2tail" else KB
            if b < 4 * nk:
                return part(w_up_2[0], half * BLOCK, KB, i * BLOCK + first + b // 4 * P + b // 2 % 2 * (FF2 * P))
            if name == "ffn2tail":
                return part(w_down_2[0], 0, nk, (b - 4 * nk) * 2 * P, 2 * P)
            return part(w_down_2[0], i * BLOCK + first, nk, (b - 4 * nk) * P)

        @block.sync
        def _(sp):
            def load(name, p, i, b, source_i):
                kt, ncols = p.shapes.get(b, (KB, P))
                s = p.slot(b)
                tensor, offset, ap = weight_source(name, source_i, b)
                freed = p.block(i, b) - REUSE + 1 + CREDIT
                sp.wait_ge(lo_dve, freed)
                sp.wait_ge(lo_pool, freed)
                sp.dma_start(w_raw[s][:, 0:kt * ncols].rearrange("p (k n) -> p k n", k=kt),
                             bass.AP(tensor=tensor, offset=offset, ap=ap)).then_inc(landed[s], 16)

            xn = Gf[:, 0:NT * D].rearrange("p (a n) -> p a n", a=NT)
            for a in range(NT):
                sp.dma_start(xn[:, a, :], x[0, a * P:(a + 1) * P, :]).then_inc(x_in, 16)

            def side(name, i, b):
                if name == "heads1" and b == 6:
                    offset = sp.snap(i * (2 * N_REL) + 1)
                    sp.wait_ge(S("scores_read1"), i * 2)
                    sp.dma_start(bias[:, :, :], bass.AP(tensor=rel_bias.tensor, offset=offset,
                                                        ap=[[1, P], [N_REL, 2], [1, NREL_COLS]])).then_inc(S("bias1_in"), 16)
                if name == "ffn1last" and b == 0:
                    sp.dma_start(Gf[:, 0:WIDTH].rearrange("p (g q) -> p g q", g=HEADS),
                                 gm_w_s_2[0].rearrange("g p q -> p g q")).then_inc(S("ws_in"), 16)
                    sp.dma_start(HS[:, 2:4, :, :].rearrange("p a b c -> p (a b c)"),
                                 bass.AP(tensor=gm_b_s_2.tensor, offset=0, ap=[[0, P], [1, WIDTH]])).then_inc(S("bs_in"), 16)
                    sp.dma_start(kTop[:, 0:64], window).then_inc(S("bs_in"), 16)
                if name == "gmv" and b == 0:
                    sp.wait_ge(S("rpb_out"), 16)
                if name == "heads2" and b == 6:
                    offset = sp.snap(i * (2 * RPB_R * RPB_C) + RPB_BACK)
                    sp.wait_ge(S("scores_read2"), i * 2)
                    for r in range(2):
                        for h in range(2):
                            sp.dma_start(
                                bias[64 * r:64 * r + 64, h, :].rearrange("p (j k) -> p j k", k=64),
                                bass.AP(tensor=rpb_back.tensor,
                                        offset=offset + (h * RPB_R * RPB_C + r * RPB_C),
                                        ap=[[1, 64], [RPB_C, 6], [1, 64]])).then_inc(S("bias2_in"), 16)

            for name, p in ph.items():
                if p.iters == 1:
                    base = {"ffn1last": FF1 // KB - 1, "ffn2last": FF2 // KB - 1}.get(name, 0)
                    for b in range(p.blocks):
                        load(name, p, 0, b, base)
                        side(name, 0, b)
                else:
                    with sp.Fori(0, p.iters) as i:
                        for b in range(p.blocks):
                            load(name, p, i, b, i)
                            side(name, i, b)
            sp.wait_ge(S("out_done"), 16 * 2 * NT)

        @block.tensor
        def _(pe):
            def products(p, i, b, bank, X, k0, first, last, nk=KB, col=0, width=P):
                s = p.slot(b)
                hi = w_hi[s][:, 0:nk * width].rearrange("p (k n) -> p k n", k=nk)
                lo = w_lo[s][:, 0:nk * width].rearrange("p (k n) -> p k n", k=nk)
                if col == 0:
                    pe.wait_ge(lo_dve, p.block(i, b) + 1 + CREDIT)
                    pe.wait_ge(lo_pool, p.block(i, b) + 1 + CREDIT)
                for k in range(nk):
                    nc.tensor.matmul(bank[:, :], hi[:, k, col:col + P], X[:, k0 + k, :],
                                     start=first and k == 0, stop=False, skip_group_check=True)
                    done = nc.tensor.matmul(bank[:, 0:T], lo[:, k, col:col + P], X[:, k0 + k, 0:T],
                                            start=False, stop=last and k == nk - 1, skip_group_check=True)
                if col + P == width:
                    done.then_inc(w_used, 1)

            def bank_free(p, i, t):
                pe.wait_ge(acc_free, p.tile(i, t) - 1 + TILE_CREDIT)

            def rms_sum(n, count, source=0, dst=psS):
                nc.tensor.matmul(dst[:, 0:T], ones[:, :], sqacc[:, source, :], start=True, stop=True).then_inc(stat_done, 1)

            pe.wait_ge(c_in, 16)
            pe.wait_ge(v_in, 16 * 11)
            nc.tensor.transpose(psT[:, 0:P], Gf[:, 4096:4096 + P], ident[:, :]).then_inc(S("vec_full"), 1)
            for t in range(4):
                done = nc.tensor.transpose(psX[:, t * 2 * FF2:(t + 1) * 2 * FF2],
                                           Gf[0:2 * FF2, 4224 + t * P:4224 + (t + 1) * P], ident[0:2 * FF2, 0:2 * FF2])
            done.then_inc(S("conv_full"), 1)
            pe.wait_ge(x_in, 16 * NT)
            xn = Gf[:, 0:NT * D].rearrange("p (a n) -> p a n", a=NT)
            banks = [psE, psA]
            for j in range(0, KD, 2):
                n = j // 2
                if n >= 2:
                    pe.wait_ge(h_ready, 2 * n - 2)
                for jj in range(2):
                    for a in range(NT):
                        done = nc.tensor.transpose(banks[n % 2][:, (jj * NT + a) * P:(jj * NT + a + 1) * P],
                                                   xn[:, a, (j + jj) * P:(j + jj + 1) * P], ident[:, :])
                done.then_inc(S("xt_full"), 1)
            pe.wait_ge(sq_added, KD)
            rms_sum(0, KD)

            p = ph["heads1"]

            def in_tiles(p, i, X, after, bank_of):
                for b in range(p.blocks):
                    t = b // 2
                    if b % 2 == 0:
                        bank_free(p, i, t)
                        if p.name == "heads1" and t == 0:
                            pe.wait_ge(S("o_rstd"), i)
                    products(p, i, b, bank_of(t), X, KB * (b % 2), b % 2 == 0, b % 2 == 1)
                    for job in after.get(b, []):
                        job(i)

            def transpose_pair(src, wait_name, full_name, read=None):
                def job(i):
                    if read is not None:
                        pe.wait_ge(S(read), i + 1)
                    pe.wait_ge(S(wait_name), i + 1)
                    for a in range(NT):
                        done = nc.tensor.transpose(psT[:, a * P:(a + 1) * P], src[:, a * P:(a + 1) * P], ident[:, :])
                    done.then_inc(S(full_name), 1)
                return job

            def decays(k):
                a, h = divmod(k, 2)
                def job(i):
                    if k == 0:
                        pe.wait_ge(S("lg_lo_ready"), i + 1)
                    else:
                        pe.wait_ge(S("decay_exp"), i * 4 + k)
                    rhs = sums[:, 4 * h + a:4 * h + a + 4, :]
                    nc.tensor.matmul(psE[:, :], lg_hi[:, a, :], rhs, start=True, stop=False)
                    nc.tensor.matmul(psE[:, :], lg_lo[:, a, :], rhs, start=False, stop=True).then_inc(S("decay_full"), 1)
                return job

            def pair_products(k):
                a, h = divmod(k, 2)
                def job(i):
                    pe.wait_ge(S("qE_ready"), i * 4 + k + 1)
                    pe.wait_ge(S("kE_ready"), i * 4 + k + 1)
                    if k:
                        pe.wait_ge(S("psA_read"), i * 4 + k)
                    for l in range(4):
                        if (k, l) in ((0, 0), (3, 3)):
                            lhsT, rhs = wk(1)[:, a * P:(a + 1) * P], wk(2)[:, a * P:(a + 1) * P]
                        else:
                            lhsT, rhs = HS[:, 2, l, :], HS[:, 1, l, :]
                        done = nc.tensor.matmul(psA[:, l * P:(l + 1) * P], lhsT, rhs, start=True, stop=True)
                    done.then_inc(S("pairs_full"), 1)
                return job

            def tile_pairs(i):
                pe.wait_ge(S("psA_read"), i * 4 + 4)
                nc.tensor.matmul(psA[:, 0:P], kTop[:, :], HS[:, 1, 3, :], start=True, stop=True).then_inc(S("top_full"), 1)

            def scan_out(i):
                pe.wait_ge(S("AT_ready"), i + 1)
                pe.wait_ge(S("top_copied"), i + 1)
                pe.wait_ge(S("v_ready"), i + 1)
                nc.tensor.matmul(psE[:, 0:T], v_nat[:, 0, :], AT[:, 0:2, :], start=True, stop=False, skip_group_check=True)
                nc.tensor.matmul(psE[:, P:T], v_nat[:, 1, :], AT[:, 2, :], start=False, stop=True,
                                 skip_group_check=True).then_inc(S("o_full"), 1)

            def scan_rms(i):
                pe.wait_ge(S("o_sq"), i + 1)
                nc.tensor.matmul(psE[:, 0:T], ones[:, :], wk(4), start=True, stop=True).then_inc(S("o_sum"), 1)

            def scores(a, nk, x):
                def job(i):
                    if a == 0:
                        pe.wait_ge(S(f"qk_ready{x}"), i + 1)
                        pe.wait_ge(S(f"yb_ready{x}"), i)
                    else:
                        pe.wait_ge(S(f"scores_read{x}"), i * 2 + 1)
                    for h, bank in enumerate((psS, psX)):
                        q0 = 64 * h
                        done = nc.tensor.matmul(bank[:, 0:nk], wk(6)[q0:q0 + 64, a * P:(a + 1) * P],
                                                wk(7)[q0:q0 + 64, 0:nk], start=True, stop=True)
                    done.then_inc(S(f"scores_full{x}"), 1)
                return job

            def prob_transposes(h, x):
                parts = [(0, 0), (0, 1), (1, 1)] if x == 1 else [(0, 0), (0, 1), (1, 0), (1, 1)]
                def job(i):
                    pe.wait_ge(S(f"probs_ready{x}"), i * 2 + 2)
                    pe.wait_ge(S(f"av_ready{x}") if h == 0 else S(f"pT_ready{x}"), i + 1 if h == 0 else i * 2 + 1)
                    for n, (k, q) in enumerate(parts):
                        done = nc.tensor.transpose(psT[:, n * P:(n + 1) * P], probs[:, q, h, k * P:(k + 1) * P], ident[:, :])
                    done.then_inc(S(f"pT_full{x}"), 1)
                return job

            def attend(h, x):
                def job(i):
                    pe.wait_ge(S(f"pT_ready{x}"), i * 2 + h + 1)
                    dst = psS[64 * h:64 * h + 64, :]
                    nc.tensor.matmul(dst[:, 0:T], av_nat[:, 0, 64 * h:64 * h + 64], pT[:, 0:2, :],
                                     start=True, stop=False, skip_group_check=True)
                    if x == 1:
                        done = nc.tensor.matmul(dst[:, P:T], av_nat[:, 1, 64 * h:64 * h + 64], pT[:, 2, :],
                                                start=False, stop=True, skip_group_check=True)
                    else:
                        done = nc.tensor.matmul(dst[:, 0:T], av_nat[:, 1, 64 * h:64 * h + 64], pT[:, 2:4, :],
                                                start=False, stop=True, skip_group_check=True)
                    done.then_inc(S(f"attended{x}"), 1)
                return job

            after1 = {
                6: [transpose_pair(wk(0), "lg_ready", "lgT_full")],
                8: [decays(0)],
                9: [transpose_pair(wk(5), "vi_ready", "vT_full")],
                10: [pair_products(0), decays(1)],
                12: [pair_products(1), decays(2)],
                13: [scores(0, P, 1)],
                14: [pair_products(2), decays(3), transpose_pair(wk(5), "avz_ready", "avT_full", "v_ready")],
                15: [scores(1, T, 1)],
                16: [pair_products(3)],
                17: [tile_pairs, prob_transposes(0, 1)],
                18: [scan_out, attend(0, 1), prob_transposes(1, 1)],
                19: [attend(1, 1)],
                20: [scan_rms],
            }
            pe.wait_ge(x_ready, KD)
            with pe.Fori(0, p.iters) as i:
                in_tiles(p, i, XU, after1, lambda t: psE if t == 0 else acc[(t - 1) % 2])

            def branches(name, n_y):
                p = ph[name]
                X = XY if name == "branch1" else XU
                x = name[-1]
                pe.wait_ge(S(f"ya_ready{x}"), HEADS)
                pe.wait_ge(S(f"yb_ready{x}"), HEADS)
                with pe.Fori(0, p.iters) as i:
                    for b in range(p.blocks):
                        bank_free(p, i, b)
                        products(p, i, b, acc[b % 2], X, KB * (b % 2), True, True)

            def out_projection(name):
                p = ph[name]
                X = XU if name == "out1" else XY
                pe.wait_ge(S(f"m_ready{name[-1]}"), KD)
                with pe.Fori(0, p.iters) as i:
                    for b in range(p.blocks):
                        if b % 2 == 0:
                            bank_free(p, i, b // 2)
                        products(p, i, b, acc[b // 2 % 2], X, KB * (b % 2), b % 2 == 0, b % 2 == 1)

            branches("branch1", 0)
            out_projection("out1")
            pe.wait_ge(sq_added, 2 * KD)
            rms_sum(1, 2 * KD)
            pe.wait_ge(x_ready, 2 * KD)

            def ffn1(p, i, n):
                for b in range(2 * KB):
                    if b % 2 == 0:
                        bank_free(p, i, b // 2)
                    products(p, i, b, acc[b // 2 % 2], XY, KB * (b % 2), b % 2 == 0, b % 2 == 1)
                pe.wait_ge(S("act1_ready"), (n + 1) * KB)
                for b in range(2 * KB, p.blocks):
                    bank_free(p, i, b - KB)
                    products(p, i, b, acc[b % 2], XU, 0, True, True)

            with pe.Fori(0, ph["ffn1"].iters) as i:
                ffn1(ph["ffn1"], i, i)
            ffn1(ph["ffn1last"], 0, ph["ffn1"].iters)

            pe.wait_ge(sq_added, 3 * KD)
            pe.wait_ge(sq2_added, KD)
            rms_sum(2, 0)
            rms_sum(2, 0, 1, psX)
            pe.wait_ge(S("ws_in"), 16)
            for g in range(HEADS):
                bank = (psE, psA)[g // 4]
                done = nc.tensor.transpose(bank[:, g % 4 * P:(g % 4 + 1) * P], Gf[:, g * P:(g + 1) * P], ident[:, :])
            done.then_inc(S("wsT_full"), 1)
            pe.wait_ge(x_ready, 3 * KD)
            pe.wait_ge(S("wsT_ready"), 2)
            p = ph["gmv"]
            for b in range(p.blocks):
                if b % 2 == 0:
                    bank_free(p, 0, b // 2)
                products(p, 0, b, acc[b // 2 % 2], XY, KB * (b % 2), b % 2 == 0, b % 2 == 1)
            for t in range(HEADS):
                pe.wait_ge(S("gv_ready"), t + 1)
                done = nc.tensor.matmul(psT[:, 0:T], ones[:, :], G[:, 24 + t, :], start=t == 0, stop=t == HEADS - 1)
            done.then_inc(S("gv_sum"), 1)
            for t in range(HEADS):
                pe.wait_ge(S("gv_sq"), t + 1)
                done = nc.tensor.matmul(psE[:, 0:T], ones[:, :], wk(t % 2), start=t == 0, stop=t == HEADS - 1)
                done.then_inc(S("gv_sq_used"), 1)

            def mix(i):
                pe.wait_ge(S("vn_ready"), i + 1)
                for n in range(NT):
                    done = nc.tensor.matmul(psA[:, n * P:(n + 1) * P], v_nat[:, n, :],
                                            HS[:, 0:2, :, :].rearrange("p a b c -> p (a b c)")[:, ds(i * P, P)],
                                            start=True, stop=True)
                done.then_inc(S("mix_full"), 1)

            after2 = {
                4: [transpose_pair(wk(3), "vh_ready", "vh_full")],
                5: [mix],
                7: [scores(0, T, 2)],
                8: [transpose_pair(wk(5), "avz_ready2", "avT_full2")],
                9: [scores(1, T, 2)],
                12: [prob_transposes(0, 2)],
                13: [attend(0, 2), prob_transposes(1, 2)],
                14: [attend(1, 2)],
            }
            p = ph["heads2"]
            with pe.Fori(0, p.iters) as i:
                in_tiles(p, i, XY, after2, lambda t: acc[t % 2])
            branches("branch2", 0)
            out_projection("out2")
            pe.wait_ge(sq_added, 4 * KD)
            rms_sum(3, 4 * KD)
            pe.wait_ge(x_ready, 4 * KD)

            def ffn2(p, i, n, finish=None):
                nk = FF2 % KB if p.name == "ffn2tail" else KB
                for b in range(4 * nk):
                    if b % 2 == 0:
                        bank_free(p, i, b // 2)
                    products(p, i, b, acc[b // 2 % 2], XU, KB * (b % 2), b % 2 == 0, b % 2 == 1)
                pe.wait_ge(S("act2_ready"), n)
                if p.name == "ffn2tail":
                    for b in range(4 * nk, p.blocks):
                        for c in range(2):
                            t = 2 * (b - 4 * nk) + c
                            bank_free(p, i, 2 * nk + t)
                            products(p, i, b, acc[t % 2], XY, 0, True, True, nk, c * P, 2 * P)
                    return
                for b in range(4 * nk, p.blocks):
                    t = b - 4 * nk
                    bank_free(p, i, 2 * nk + t)
                    products(p, i, b, acc[t % 2], XY, 0, True, True)
                    if finish is not None and t >= 1:
                        finish(t - 1)

            def output_transposes(j):
                pe.wait_ge(S("hw_ready"), j + 1)
                bank = (psE, psA)[j % 2]
                if j >= 2:
                    pe.wait_ge(S("out_copied"), j - 1)
                for a in range(NT):
                    done = nc.tensor.transpose(bank[:, a * P:(a + 1) * P], sqb[:, j % 2, a * P:(a + 1) * P], ident[:, :])
                done.then_inc(S("outT_full"), 1)

            ffn2(ph["ffn2tail"], 0, FF2 % KB)
            with pe.Fori(0, ph["ffn2"].iters) as i:
                ffn2(ph["ffn2"], i, i * KB + (FF2 % KB + KB))
            ffn2(ph["ffn2last"], 0, FF2, output_transposes)
            output_transposes(KD - 1)
            pe.wait_ge(S("sqf_added"), KD)
            for a in range(NT):
                done = nc.tensor.matmul(psT[:, a:a + 1], sqacc[:, 0, a * P:(a + 1) * P], ones[:, 0:1], start=True, stop=True)
            done.then_inc(S("out_sum"), 1)

        @block.scalar
        def _(act):
            link = Link(act, act_step)
            act.dma_start(ident[:, :], identity).then_inc(c_in, 16)
            for n, v in enumerate((norm_mix_w, norm_mlp_w, norm_final_w, norm_mix_2, norm_ffn_2, norm_final_2)):
                src = v[0] if len(v.shape) == 2 else v
                act.dma_start(Gf[16 * n:16 * n + 16, 4096:4096 + P], src.rearrange("(j p) -> j p", p=P)).then_inc(v_in, 16)
            act.dma_start(Gf[96:112, 4096:4096 + P], lb_logits.rearrange("l (j p) -> (l j) p", p=P)).then_inc(v_in, 16)
            act.dma_start(Gf[112:120, 4096:4096 + P], gm_ln_g_2[0].rearrange("(j p) -> j p", p=P)).then_inc(v_in, 16)
            act.dma_start(Gf[120:128, 4096:4096 + P], gm_ln_b_2[0].rearrange("(j p) -> j p", p=P)).then_inc(v_in, 16)
            act.dma_start(Gf[0:2 * FF2, 4224:4224 + 3 * P].rearrange("j (t p) -> j t p", t=3),
                          conv_k_2[0].rearrange("t (j p) -> j t p", p=P)).then_inc(v_in, 16)
            act.dma_start(Gf[0:2 * FF2, 4224 + 3 * P:4224 + 4 * P], conv_b_2[0].rearrange("(j p) -> j p", p=P)).then_inc(v_in, 16)
            act.dma_start(hgw, hg_norm_w.rearrange("a p -> p a")).then_inc(S("hgw_in"), 16)
            act.dma_start(Gf[:, 4736:4736 + 9 * P], range_sums).then_inc(S("sums_in"), 16)
            act.dma_start(Gf[:, 5888:5888 + 9 * P], pair_masks).then_inc(S("masks_in"), 16)

            rpb_in = Gf[0:2 * HEADS, 7040:7040 + RPB_R * RPB_C]
            rpb_turned = Gf[0:2 * HEADS, 7552:7552 + RPB_R * RPB_C]
            act.dma_start(rpb_in, na_rpb_2[0].rearrange("h r c -> h (r c)")).then_inc(S("rpb_in"), 16)

            def round_block(p, i, b):
                c = b + LEAD
                if p is last_phase and c >= p.blocks:
                    return
                s, n = p.slot(c), (p.size(c) if c < p.blocks else BLOCK)
                act.wait_ge(landed[s], p.landed(i, c))
                act.wait_ge(w_used, p.block(i, b) + 1)
                act.activation(w_hi[s][:, 0:n], w_raw[s][:, 0:n], ACT.Copy).then_inc(hi_done, 1)

            def copy_cross(p, i, c, b, bank):
                act.wait_ge(w_used, p.block(i, b) + 1)
                act.activation(cross[:, c % 2, :], bank[:, T:2 * T], ACT.Copy).then_inc(cross_ready, 1)

            def rstd(dst, src, width, eps, tmp, done):
                link(act.activation(tmp, src, ACT.Ln, bias=eps, scale=1.0 / width))
                act.activation(dst, tmp, ACT.Exp, scale=-0.5).then_inc(done, 1)

            act.wait_ge(lo_dve, CREDIT)
            for b in range(LEAD):
                act.wait_ge(landed[b], 16)
                act.activation(w_hi[b][:, :], w_raw[b][:, :], ACT.Copy).then_inc(hi_done, 1)
            act.wait_ge(S("sums_in"), 16)
            link(act.activation(sums[:, :, :].rearrange("p a b -> p (a b)"), Gf[:, 4736:4736 + 9 * P], ACT.Copy))
            act.wait_ge(S("masks_in"), 16)
            link(act.activation(masks[:, :, :].rearrange("p a b -> p (a b)"), Gf[:, 5888:5888 + 9 * P], ACT.Copy))
            act.wait_ge(S("rpb_in"), 16)
            act.activation(rpb_turned, Gf[0:2 * HEADS, 7040 + RPB_R * RPB_C - 1:7039:-1], ACT.Copy).then_inc(S("rpb_turned"), 1)
            act.wait_ge(S("rpb_turned"), 1)
            act.dma_start(rpb_back, rpb_turned).then_inc(S("rpb_out"), 16)
            act.wait_ge(S("lb_max"), 1)
            act.activation(lbt[:, 0:16], lbt[:, 0:16], ACT.Exp).then_inc(S("lb_exp"), 1)
            for j in range(KD):
                act.wait_ge(h_ready, j + 1)
                if j:
                    act.wait_ge(sq_added, j)
                act.activation(sqb[:, j % 2, :], hT[:, j, :], ACT.Square).then_inc(sq_ready, 1)
                act.activation(XU[:, j, 0:T], hT[:, j, :], ACT.Copy, scale=cols[:, C_MIX1 + j:C_MIX1 + j + 1]).then_inc(uh_ready, 1)
            act.wait_ge(stat_done, 1)
            rstd(rs[:, :], psS[:, 0:T], D, eps_rms, rs1[:, :], rs_ready)

            def sigmoid_of(n, wait_name, done_name, i):
                act.wait_ge(S(wait_name), i + 1)
                act.activation(wk(4), wk(n), ACT.Sigmoid).then_inc(S(done_name), 1)

            def softmax_exp(a, nk, x, i):
                act.wait_ge(S(f"max_ready{x}"), i * 2 + a + 1)
                for h in range(2):
                    ins = act.activation(probs[:, a, h, 0:nk], probs[:, a, h, 0:nk], ACT.Exp,
                                         bias=soft[:, 1, a, h:h + 1], accum_out=soft[:, 2, a, h:h + 1])
                    ins.then_inc(S(f"exp_done{x}"), 1)

            def evac_pT(h, x, i):
                n = 3 if x == 1 else 4
                act.wait_ge(S(f"pT_full{x}"), i * 2 + h + 1)
                if h == 1:
                    act.wait_ge(S(f"attended{x}"), i * 2 + 1)
                act.activation(pT[:, 0:n, :], psT[:, 0:n * P], ACT.Copy).then_inc(S(f"pT_ready{x}"), 1)

            def high_of_attention(x, i, X):
                act.wait_ge(S(f"attended{x}"), i * 2 + 2)
                act.activation(X[:, ds(i + HEADS, 1), 0:T], psS[:, 0:T].rearrange("p (a t) -> p a t", a=1),
                               ACT.Copy).then_inc(S(f"ybh_ready{x}"), 1)

            def gates_sigmoid(x, i):
                act.wait_ge(S(f"gates_z{x}"), i + 1)
                act.activation(G[:, ds(i * 4, 4), :], G[:, ds(i * 4, 4), :], ACT.Sigmoid).then_inc(S(f"gates_ready{x}"), 1)

            p = ph["heads1"]
            with act.Fori(0, p.iters) as i:
                link.enter(i, 1)
                for b in range(p.blocks):
                    round_block(p, i, b)
                    t = b // 2
                    if b % 2:
                        copy_cross(p, i, t, b, psE if t == 0 else acc[(t - 1) % 2])
                    if b == 1:
                        sigmoid_of(2, "hq_z", "hq_sig", i)
                    if b == 3:
                        act.wait_ge(S("q_ready"), i + 1)
                        sigmoid_of(0, "hf_z", "hf_sig", i)
                    if b == 5:
                        act.wait_ge(S("g_ready"), i + 1)
                        sigmoid_of(3, "hg_z", "hg_sig", i)
                        act.activation(wk(0), wk(0), ACT.Ln).then_inc(S("lg_ready"), 1)
                    if b == 6:
                        act.wait_ge(S("lgT_full"), i + 1)
                        act.activation(lg_hi[:, :, :], psT[:, 0:T], ACT.Copy).then_inc(S("lg_hi_ready"), 1)
                    if b in (8, 10, 12, 14):
                        k = (b - 8) // 2
                        act.wait_ge(S("decay_full"), i * 4 + k + 1)
                        if k:
                            act.wait_ge(S("qE_ready"), i * 4 + k)
                            act.wait_ge(S("kE_ready"), i * 4 + k)
                        act.activation(HS[:, 0, :, :], psE[:, :], ACT.Exp).then_inc(S("decay_exp"), 1)
                    if b == 9:
                        act.wait_ge(S("vT_full"), i + 1)
                        act.activation(v_nat[:, :, :], psT[:, 0:T], ACT.Copy).then_inc(S("v_ready"), 1)
                    if b == 14:
                        act.wait_ge(S("avT_full"), i + 1)
                        act.activation(av_nat[:, :, :], psT[:, 0:T], ACT.Copy).then_inc(S("av_ready1"), 1)
                    if b == 13:
                        softmax_exp(0, P, 1, i)
                    if b == 15:
                        softmax_exp(1, T, 1, i)
                    if b == 17:
                        act.wait_ge(S("top_full"), i + 1)
                        act.activation(AT[:, 1, :], psA[:, 0:P], ACT.Copy).then_inc(S("top_copied"), 1)
                        evac_pT(0, 1, i)
                    if b == 18:
                        act.wait_ge(S("o_full"), i + 1)
                        act.activation(wk(0), psE[:, 0:T], ACT.Copy).then_inc(S("o_copied"), 1)
                        evac_pT(1, 1, i)
                    if b == 19:
                        high_of_attention(1, i, XY)
                    if b == 20:
                        act.wait_ge(S("o_sum"), i + 1)
                        link(act.activation(wk(5), psE[:, 0:T], ACT.Ln, bias=eps_rms, scale=1.0 / P))
                        act.activation(wk(5), wk(5), ACT.Exp, scale=-0.5).then_inc(S("o_rstd"), 1)
                    if b == 21:
                        act.wait_ge(S("ya_z1"), i + 1)
                        act.activation(XY[:, ds(i, 1), 0:T], work[:, 0:1, 0:T], ACT.Copy).then_inc(S("yah_ready1"), 1)
                        gates_sigmoid(1, i)
                link.leave(p.iters)

            def branches(name, X):
                p, x = ph[name], name[-1]
                with act.Fori(0, p.iters) as i:
                    for b in range(p.blocks):
                        round_block(p, i, b)
                        copy_cross(p, i, b, b, acc[b % 2])
                        if b % 2:
                            act.wait_ge(S(f"mz_ready{x}"), i * 8 + b // 2 + 1)
                            act.activation(X[:, ds(i * 8 + b // 2, 1), 0:T], work[:, 0:1, 0:T], ACT.Copy)\
                               .then_inc(S(f"mh_ready{x}"), 1)

            def operand_tile(n, X, j, wcol, p, i, t):
                act.wait_ge(acc_free, p.tile(i, t) + 1 + TILE_CREDIT)
                act.wait_ge(sq_added, n)
                act.activation(sqb[:, 0:1, :], hT[:, ds(j, 1), :], ACT.Square).then_inc(sq_ready, 1)
                act.activation(X[:, ds(j, 1), 0:T], hT[:, ds(j, 1), :], ACT.Copy, scale=wcol).then_inc(uh_ready, 1)

            def out_projection(name, X, n0, c0):
                p = ph[name]
                with act.Fori(0, p.iters) as i:
                    for b in range(p.blocks):
                        round_block(p, i, b)
                        if b % 2:
                            j = i * 8 + b // 2
                            operand_tile(n0 * KD + j, X, j, cols[:, ds(j + c0, 1)], p, i, b // 2)

            branches("branch1", XU)
            out_projection("out1", XY, 1, C_MLP1)
            act.wait_ge(stat_done, 2)
            rstd(rs[:, :], psS[:, 0:T], D, eps_rms, rs1[:, :], rs_ready)

            def ffn1(p, i, n, last):
                for b in range(p.blocks):
                    round_block(p, i, b)
                    if b < 2 * KB and b % 2:
                        t = b // 2
                        copy_cross(p, i, t, b, acc[t % 2])
                        act.wait_ge(S("act1_z"), n * KB + t + 1)
                        act.activation(XU[:, t, 0:T], wk(1), ACT.Copy).then_inc(S("act1_hi"), 1)
                    if last and b >= 2 * KB:
                        j = b - 2 * KB
                        operand_tile(2 * KD + j, XY, j, fm2[:, j:j + 1], p, i, KB + j)
                        if j:
                            act.wait_ge(sq2_added, j)
                        act.activation(sqb[:, 1, :], hT[:, j, :], ACT.Square,
                                       scale=cols[:, C_FIN1 + j:C_FIN1 + j + 1]).then_inc(sq2_ready, 1)

            with act.Fori(0, ph["ffn1"].iters) as i:
                ffn1(ph["ffn1"], i, i, False)
            ffn1(ph["ffn1last"], 0, ph["ffn1"].iters, True)

            act.wait_ge(stat_done, 3)
            link(act.activation(rs[:, :], psS[:, 0:T], ACT.Ln, bias=eps_rms, scale=1.0 / D))
            act.activation(rs1[:, :], rs[:, :], ACT.Exp, scale=-0.5).then_inc(S("rs1_ready"), 1)
            act.wait_ge(S("ms2_ready"), 1)
            link(act.activation(rs[:, :], wk(8), ACT.Ln, bias=eps_rms, scale=1.0 / D))
            act.activation(rs[:, :], rs[:, :], ACT.Exp, scale=-0.5).then_inc(rs_ready, 1)
            act.wait_ge(S("wsT_full"), 1)
            for g, bank in enumerate((psE, psA)):
                act.activation(HS[:, g, :, :], bank[:, :], ACT.Copy).then_inc(S("wsT_ready"), 1)

            p = ph["gmv"]
            for b in range(p.blocks):
                round_block(p, 0, b)
                if b % 2:
                    t = b // 2
                    copy_cross(p, 0, t, b, acc[t % 2])
                    act.wait_ge(S("gv_z"), t + 1)
                    act.activation(G[:, 24 + t, :], G[:, 24 + t, :], ACT.Gelu_apprx_tanh).then_inc(S("gv_ready"), 1)
            act.wait_ge(S("gv_sq_used"), HEADS)
            rstd(rs1[:, :], psE[:, 0:T], WIDTH, eps_ln, wk(4), S("gv_rstd"))

            p = ph["heads2"]
            with act.Fori(0, p.iters) as i:
                for b in range(p.blocks):
                    round_block(p, i, b)
                    t = b // 2
                    if b % 2:
                        copy_cross(p, i, t, b, acc[t % 2])
                    if b == 1:
                        act.wait_ge(S("u_z"), i + 1)
                        act.activation(wk(0), wk(0), ACT.Gelu_apprx_tanh).then_inc(S("u_ready"), 1)
                    if b == 4:
                        act.wait_ge(S("vh_full"), i + 1)
                        act.activation(v_nat[:, :, :], psT[:, 0:T], ACT.Copy).then_inc(S("vn_ready"), 1)
                    if b == 6:
                        act.wait_ge(S("ya_z2"), i + 1)
                        act.activation(XU[:, ds(i, 1), 0:T], work[:, 1:2, 0:T], ACT.Copy).then_inc(S("yah_ready2"), 1)
                    if b == 8:
                        act.wait_ge(S("avT_full2"), i + 1)
                        act.activation(av_nat[:, :, :], psT[:, 0:T], ACT.Copy).then_inc(S("av_ready2"), 1)
                    if b == 7:
                        softmax_exp(0, T, 2, i)
                    if b == 9:
                        softmax_exp(1, T, 2, i)
                    if b == 12:
                        evac_pT(0, 2, i)
                    if b == 13:
                        evac_pT(1, 2, i)
                    if b == 14:
                        high_of_attention(2, i, XU)
                    if b == 15:
                        gates_sigmoid(2, i)

            branches("branch2", XY)
            out_projection("out2", XU, 3, C_FFN2)
            act.wait_ge(stat_done, 5)
            rstd(rs[:, :], psS[:, 0:T], D, eps_rms, rs1[:, :], rs_ready)

            def ffn2(p, i, n, f0, last):
                nk = FF2 % KB if p.name == "ffn2tail" else KB
                for b in range(p.blocks):
                    round_block(p, i, b)
                    if b < 4 * nk and b % 2:
                        t, val = divmod(b // 2, 2)
                        copy_cross(p, i, b // 2, b, acc[b // 2 % 2])
                        act.wait_ge(S("conv_z"), (n + t) * 2 + val + 1)
                        ch = f0 + t + val * FF2
                        act.activation(wk(2 + val), work[:, val, 0:T], ACT.Identity, scale=convc[:, 0, ds(ch, 1)],
                                       bias=convc[:, 3, ds(ch, 1)]).then_inc(S("conv_first"), 1)
                        if val == 0:
                            act.wait_ge(S("gate_conv"), n + t + 1)
                            act.activation(wk(4), wk(2), ACT.Silu).then_inc(S("gate_silu"), 1)
                        else:
                            act.wait_ge(S("act2_z"), n + t + 1)
                            act.activation(XY[:, t, 0:T], wk(5), ACT.Copy).then_inc(S("act2_hi"), 1)
                    if last and b >= 4 * nk:
                        j = b - 4 * nk
                        act.wait_ge(acc_free, p.tile(i, 2 * nk + j) + 1 + TILE_CREDIT)
                        if j >= 2:
                            act.wait_ge(S("outT_full"), j - 1)
                        act.activation(sqb[:, j % 2, :], hT[:, j, :], ACT.Copy,
                                       scale=cols[:, C_FIN2 + j:C_FIN2 + j + 1]).then_inc(S("hw_ready"), 1)
                        if j >= 2:
                            act.wait_ge(S("sqf_added"), j - 1)
                        act.activation(wk(6 + j % 2), hT[:, j, :], ACT.Square).then_inc(S("sqf_ready"), 1)

            ffn2(ph["ffn2tail"], 0, 0, 0, False)
            with act.Fori(0, ph["ffn2"].iters) as i:
                ffn2(ph["ffn2"], i, i * KB + FF2 % KB, i * KB + FF2 % KB, False)
            ffn2(ph["ffn2last"], 0, FF2 - KB, FF2 - KB, True)

            act.wait_ge(S("out_sum"), 1)
            link(act.activation(small[:, 4:6], psT[:, 0:NT], ACT.Ln, bias=eps_rms, scale=1.0 / D))
            act.activation(small[:, 6:8], small[:, 4:6], ACT.Exp, scale=-0.5).then_inc(S("out_rstd"), 1)
            act.wait_ge(S("out_rstd"), 1)
            act.wait_ge(S("out_copied"), KD)
            for c in range(2):
                part = Gf[:, D + c * D // 2:D + (c + 1) * D // 2]
                act.activation(part, part, ACT.Copy, scale=small[:, 7:8]).then_inc(S("out_scaled1"), 1)
                act.wait_ge(S("out_scaled1"), c + 1)
                act.dma_start(out[0, P:2 * P, c * D // 2:(c + 1) * D // 2], part).then_inc(S("out_done"), 16)
            for c in range(2):
                act.wait_ge(S("out_scaled0"), c + 1)
                act.dma_start(out[0, 0:P, c * D // 2:(c + 1) * D // 2], Gf[:, c * D // 2:(c + 1) * D // 2])\
                   .then_inc(S("out_done"), 16)

        @block.gpsimd
        def _(pool):
            def low_part(p, i, b):
                c = b + LEAD
                if p is last_phase and c >= p.blocks:
                    return
                s, n = p.slot(c), (p.size(c) if c < p.blocks else BLOCK)
                pool.wait_ge(hi_done, p.block(i, c) + 1)
                nc.gpsimd.tensor_tensor(w_lo[s][:, n // 2:n], w_raw[s][:, n // 2:n], w_hi[s][:, n // 2:n].bitcast(F32),
                                        ALU.subtract).then_inc(lo_pool, 1)

            def add_square(n):
                pool.wait_ge(sq_ready, n + 1)
                nc.gpsimd.tensor_tensor(sqacc[:, 0, :], sqacc[:, 0, :], sqb[:, 0, :], ALU.add).then_inc(sq_added, 1)
                pool.wait_ge(sq_added, n + 1)

            def clear_sums():
                nc.gpsimd.memset(sqacc[:, :, :], 0.0).then_inc(S("sums_cleared"), 1)
                cleared[0] += 1
                pool.wait_ge(S("sums_cleared"), cleared[0])

            cleared = [0]
            for n in range(CREDIT):
                nc.gpsimd.memset(ones[:, n * 32:(n + 1) * 32], 1.0).then_inc(lo_pool, 1)
            clear_sums()
            for b in range(LEAD):
                pool.wait_ge(hi_done, b + 1)
                nc.gpsimd.tensor_tensor(w_lo[b][:, BLOCK // 2:], w_raw[b][:, BLOCK // 2:], w_hi[b][:, BLOCK // 2:].bitcast(F32),
                                        ALU.subtract).then_inc(lo_pool, 1)
            for j in range(KD):
                pool.wait_ge(sq_ready, j + 1)
                nc.gpsimd.tensor_tensor(sqacc[:, 0, :], sqacc[:, 0, :], sqb[:, j % 2, :], ALU.add).then_inc(sq_added, 1)
                pool.wait_ge(sq_added, j + 1)

            p = ph["heads1"]
            with pool.Fori(0, p.iters) as i:
                for b in range(p.blocks):
                    low_part(p, i, b)
                    if b in (8, 10, 12, 14):
                        k = (b - 8) // 2
                        pool.wait_ge(S("decay_exp"), i * 4 + k + 1)
                        if k == 0:
                            pool.wait_ge(S("g_ready"), i + 1)
                        else:
                            pool.wait_ge(S("pairs_full"), i * 4 + k)
                        kk = wk(1)[:, (k // 2) * P:(k // 2 + 1) * P].rearrange("p (a t) -> p a t", a=1)
                        nc.gpsimd.tensor_tensor(HS[:, 2, :, :], HS[:, 0, :, :], kk.to_broadcast([P, 4, P]), ALU.mult)\
                          .then_inc(S("kE_ready"), 1)

            def plain(name):
                p = ph[name]
                if p.iters == 1:
                    for b in range(p.blocks):
                        low_part(p, 0, b)
                else:
                    with pool.Fori(0, p.iters) as i:
                        for b in range(p.blocks):
                            low_part(p, i, b)

            def out_projection(name, n0):
                p = ph[name]
                with pool.Fori(0, p.iters) as i:
                    for b in range(p.blocks):
                        low_part(p, i, b)
                        if b % 2:
                            add_square(i * 8 + (n0 * KD + b // 2))

            plain("branch1")
            pool.wait_ge(stat_done, 1)
            clear_sums()
            out_projection("out1", 1)
            plain("ffn1")
            pool.wait_ge(stat_done, 2)
            clear_sums()
            p = ph["ffn1last"]
            for b in range(p.blocks):
                low_part(p, 0, b)
                if b >= 2 * KB:
                    j = b - 2 * KB
                    add_square(2 * KD + j)
                    pool.wait_ge(sq2_ready, j + 1)
                    nc.gpsimd.tensor_tensor(sqacc[:, 1, :], sqacc[:, 1, :], sqb[:, 1, :], ALU.add).then_inc(sq2_added, 1)
                    pool.wait_ge(sq2_added, j + 1)
            plain("gmv")
            plain("heads2")
            plain("branch2")
            pool.wait_ge(stat_done, 4)
            clear_sums()
            out_projection("out2", 3)
            plain("ffn2tail")
            plain("ffn2")
            pool.wait_ge(stat_done, 5)
            clear_sums()
            p = ph["ffn2last"]
            for b in range(p.blocks):
                low_part(p, 0, b)
                if b >= 4 * KB:
                    j = b - 4 * KB
                    pool.wait_ge(S("sqf_ready"), j + 1)
                    nc.gpsimd.tensor_tensor(sqacc[:, 0, :], sqacc[:, 0, :], wk(6 + j % 2), ALU.add).then_inc(S("sqf_added"), 1)
                    pool.wait_ge(S("sqf_added"), j + 1)

        @block.vector
        def _(dve):
            link = Link(dve, dve_step)
            V = nc.vector

            def mark(ins, s, value):
                ins.then_inc(s, 1)
                dve.wait_ge(s, value)

            def low_part(p, i, b):
                c = b + LEAD
                if p is last_phase and c >= p.blocks:
                    return
                s, n = p.slot(c), (p.size(c) if c < p.blocks else BLOCK)
                dve.wait_ge(hi_done, p.block(i, c) + 1)
                V.tensor_tensor(w_lo[s][:, 0:n // 2], w_raw[s][:, 0:n // 2], w_hi[s][:, 0:n // 2].bitcast(F32),
                                ALU.subtract).then_inc(lo_dve, 1)

            def tile_sum(p, i, c, b, t, bank, dst):
                dve.wait_ge(cross_ready, p.cross(i, c) + 1)
                mark(V.tensor_tensor(dst, bank[:, 0:T], cross[:, c % 2, :], ALU.add), acc_free,
                     p.tile(i, t) + 1 + TILE_CREDIT)

            def scaled_tile(p, i, c, b, t, bank, dst, s, value):
                tile_sum(p, i, c, b, t, bank, dst)
                mark(V.tensor_tensor(dst, dst, rs[:, :], ALU.mult), s, value)

            for n, (dst, value) in enumerate(((eps_rms, RMS_EPS), (eps_ln, LN_EPS), (small[:, 3:4], 0.0), (small[:, 4:5], 0.0))):
                V.memset(dst, value).then_inc(lo_dve, 1)
            for n in range(TILE_CREDIT):
                V.memset(small[:, 5 + n:6 + n], 0.0).then_inc(acc_free, 1)
            dve.wait_ge(lo_dve, CREDIT)
            dve.wait_ge(acc_free, TILE_CREDIT)
            for b in range(LEAD):
                dve.wait_ge(hi_done, b + 1)
                V.tensor_tensor(w_lo[b][:, 0:BLOCK // 2], w_raw[b][:, 0:BLOCK // 2], w_hi[b][:, 0:BLOCK // 2].bitcast(F32),
                                ALU.subtract).then_inc(lo_dve, 1)
            dve.wait_ge(S("vec_full"), 1)
            mark(V.tensor_copy(cols[:, :], psT[:, 0:P]), S("cols_ready"), 1)
            link(V.tensor_tensor(lbt[:, 16:24], cols[:, C_LB:C_LB + 8], cols[:, C_LB + 8:C_LB + 16], ALU.max))
            link(V.tensor_tensor(lbt[:, 0:8], cols[:, C_LB:C_LB + 8], lbt[:, 16:24], ALU.subtract))
            mark(V.tensor_tensor(lbt[:, 8:16], cols[:, C_LB + 8:C_LB + 16], lbt[:, 16:24], ALU.subtract), S("lb_max"), 1)
            dve.wait_ge(S("lb_exp"), 1)
            link(V.tensor_tensor(lbt[:, 16:24], lbt[:, 0:8], lbt[:, 8:16], ALU.add))
            link(V.reciprocal(lbt[:, 16:24], lbt[:, 16:24]))
            link(V.tensor_tensor(lbc, lbt[:, 0:8], lbt[:, 16:24], ALU.mult))
            link(V.tensor_tensor(omlb, lbt[:, 8:16], lbt[:, 16:24], ALU.mult))
            link(V.tensor_tensor(fm2, cols[:, C_FIN1:C_FIN1 + KD], cols[:, C_MIX2:C_MIX2 + KD], ALU.mult))
            banks = (psE, psA)

            def first_low(j):
                dve.wait_ge(uh_ready, j + 1)
                V.scalar_tensor_tensor(XU[:, j, T:2 * T], hT[:, j, :], cols[:, C_MIX1 + j:C_MIX1 + j + 1],
                                       XU[:, j, 0:T].bitcast(F32), ALU.mult, ALU.subtract).then_inc(x_ready, 1)

            for j in range(0, KD, 2):
                dve.wait_ge(S("xt_full"), j // 2 + 1)
                V.tensor_copy(hT[:, j, :], banks[j // 2 % 2][:, 0:T]).then_inc(h_ready, 1)
                mark(V.tensor_copy(hT[:, j + 1, :], banks[j // 2 % 2][:, T:2 * T]), h_ready, j + 2)
                if j:
                    first_low(j - 2)
                    first_low(j - 1)
            first_low(KD - 2)
            first_low(KD - 1)
            dve.wait_ge(S("conv_full"), 1)
            link(V.tensor_copy(convc[:, :, :], psX[:, 0:8 * FF2].rearrange("p (t j) -> p t j", t=4)))

            def softmax_front(a, nk, x, i):
                dve.wait_ge(S(f"scores_full{x}"), i * 2 + a + 1)
                for h, bank in enumerate((psS, psX)):
                    c1 = P * a + T - 1
                    rel = bias[:, h, c1:(c1 - nk if c1 >= nk else None):-1]
                    link(V.scalar_tensor_tensor(probs[:, a, h, 0:nk], bank[:, 0:nk], AT_SCALE, rel, ALU.mult, ALU.add))
                mark(V.reduce_max(soft[:, 0, a, :], probs[:, a, :, 0:nk], AX_X), S(f"scores_read{x}"), i * 2 + a + 1)
                mark(V.tensor_scalar(soft[:, 1, a, :], soft[:, 0, a, :], -1.0, None, ALU.mult), S(f"max_ready{x}"), i * 2 + a + 1)

            def softmax_back(a, nk, x, i):
                dve.wait_ge(S(f"exp_done{x}"), i * 4 + 2 * a + 2)
                link(V.reciprocal(soft[:, 3, a, :], soft[:, 2, a, :]))
                link(V.tensor_scalar(probs[:, a, 0, 0:nk], probs[:, a, 0, 0:nk], soft[:, 3, a, 0:1], None, ALU.mult))
                mark(V.tensor_scalar(probs[:, a, 1, 0:nk], probs[:, a, 1, 0:nk], soft[:, 3, a, 1:2], None, ALU.mult),
                     S(f"probs_ready{x}"), i * 2 + a + 1)

            def low_of_attention(x, i, X):
                dve.wait_ge(S(f"ybh_ready{x}"), i + 1)
                mark(V.tensor_tensor(X[:, ds(i + HEADS, 1), T:2 * T], psS[:, 0:T].rearrange("p (a t) -> p a t", a=1),
                                     X[:, ds(i + HEADS, 1), 0:T].bitcast(F32), ALU.subtract), S(f"yb_ready{x}"), i + 1)

            p = ph["heads1"]
            dve.wait_ge(rs_ready, 1)
            dve.wait_ge(S("rpb_out"), 16)
            with dve.Fori(0, p.iters) as i:
                link.enter(i, PER_HEADS1)
                for b in range(p.blocks):
                    low_part(p, i, b)
                    t = b // 2
                    bank = psE if t == 0 else acc[(t - 1) % 2]
                    if b == 1:
                        scaled_tile(p, i, 0, b, 0, bank, wk(2), S("hq_z"), i + 1)
                    if b == 2:
                        dve.wait_ge(S("hq_sig"), i + 1)
                        mark(V.scalar_tensor_tensor(wk(2), wk(2), HG_SCALE, wk(4), ALU.mult, ALU.mult), S("q_ready"), i + 1)
                    if b == 3:
                        scaled_tile(p, i, 1, b, 1, bank, wk(0), S("hf_z"), i + 1)
                    if b == 4:
                        dve.wait_ge(S("hf_sig"), i + 1)
                        link(V.tensor_scalar(wk(0), wk(4), omlb[:, ds(i, 1)], lbc[:, ds(i, 1)], ALU.mult, ALU.add))
                        mark(V.tensor_scalar(wk(1), wk(0), -1.0, 1.0, ALU.mult, ALU.add), S("g_ready"), i + 1)
                    if b == 5:
                        scaled_tile(p, i, 2, b, 2, bank, wk(3), S("hg_z"), i + 1)
                    if b == 6:
                        dve.wait_ge(S("hg_sig"), i + 1)
                        link(V.scalar_tensor_tensor(wk(3), wk(3), hgw, wk(4), ALU.mult, ALU.mult))
                        dve.wait_ge(S("lg_hi_ready"), i + 1)
                        mark(V.tensor_tensor(lg_lo[:, :, :], psT[:, 0:T].rearrange("p (a k) -> p a k", a=NT),
                                             lg_hi[:, :, :].bitcast(F32), ALU.subtract), S("lg_lo_ready"), i + 1)
                    if b == 7:
                        scaled_tile(p, i, 3, b, 3, bank, wk(5), S("vi_ready"), i + 1)
                    if b == 8:
                        dve.wait_ge(S("bias1_in"), 16 * i + 16)
                        link(V.memset(bias[0:64, :, P:P + 64], MASKED))
                    if b in (8, 10, 12, 14):
                        k = (b - 8) // 2
                        dve.wait_ge(S("decay_exp"), i * 4 + k + 1)
                        if k:
                            dve.wait_ge(S("pairs_full"), i * 4 + k)
                        q = wk(2)[:, (k // 2) * P:(k // 2 + 1) * P].rearrange("p (a t) -> p a t", a=1)
                        if k == 0:
                            link(V.tensor_tensor(kTop[:, :], HS[:, 0, 0, :], wk(1)[:, 0:P], ALU.mult))
                        mark(V.tensor_tensor(HS[:, 1, :, :], HS[:, 0, :, :], q.to_broadcast([P, 4, P]), ALU.mult),
                             S("qE_ready"), i * 4 + k + 1)
                    if b == 9:
                        scaled_tile(p, i, 4, b, 4, bank, wk(7), S("k_z"), i + 1)
                    if b in (10, 12, 14, 16):
                        k = (b - 10) // 2
                        a, h = divmod(k, 2)
                        dve.wait_ge(S("pairs_full"), i * 4 + k + 1)
                        m0 = 4 * h + a
                        mark(V.tensor_tensor(HS[:, 3, :, :], psA[:, :].rearrange("p (l t) -> p l t", l=4),
                                             masks[:, m0:m0 + 4, :], ALU.mult), S("psA_read"), i * 4 + k + 1)
                        dst = AT[:, 2 * a, :] if h == 0 else wk(8)[:, 0:P]
                        link(V.tensor_reduce(dst, HS[:, 3, :, :].rearrange("p l t -> p t l"), AX_X, ALU.add))
                        if h:
                            ins = V.tensor_tensor(AT[:, 2 * a, :], AT[:, 2 * a, :], wk(8)[:, 0:P], ALU.add)
                            if a:
                                mark(ins, S("AT_ready"), i + 1)
                            else:
                                link(ins)
                    if b == 11:
                        scaled_tile(p, i, 5, b, 5, bank, wk(6), S("qk_ready1"), i + 1)
                    if b == 13:
                        scaled_tile(p, i, 6, b, 6, bank, wk(5), S("avz_ready"), i + 1)
                        softmax_front(0, P, 1, i)
                    if b == 14:
                        softmax_back(0, P, 1, i)
                    if b == 15:
                        tile_sum(p, i, 7, b, 7, bank, wk(8))
                        link(V.tensor_tensor(G[:, ds(i * 4, 1), :], work[:, 8:9, 0:T], rs[:, :].rearrange("p (a t) -> p a t", a=1), ALU.mult))
                        softmax_front(1, T, 1, i)
                    if b == 16:
                        softmax_back(1, T, 1, i)
                    if b in (17, 19, 21):
                        n = (b - 15) // 2
                        tile_sum(p, i, 7 + n, b, 7 + n, bank, wk(8))
                        ins = V.tensor_tensor(G[:, ds(i * 4 + n, 1), :], work[:, 8:9, 0:T],
                                              rs[:, :].rearrange("p (a t) -> p a t", a=1), ALU.mult)
                        if n == 3:
                            mark(ins, S("gates_z1"), i + 1)
                        else:
                            link(ins)
                    if b == 18:
                        dve.wait_ge(S("o_copied"), i + 1)
                        mark(V.tensor_tensor(wk(4), wk(0), wk(0), ALU.mult), S("o_sq"), i + 1)
                    if b == 19:
                        low_of_attention(1, i, XY)
                    if b == 20:
                        dve.wait_ge(S("o_rstd"), i + 1)
                        link(V.tensor_tensor(wk(0), wk(0), wk(5), ALU.mult))
                        mark(V.tensor_tensor(wk(0), wk(0), wk(3), ALU.mult), S("ya_z1"), i + 1)
                    if b == 21:
                        dve.wait_ge(S("yah_ready1"), i + 1)
                        mark(V.tensor_tensor(XY[:, ds(i, 1), T:2 * T], work[:, 0:1, 0:T],
                                             XY[:, ds(i, 1), 0:T].bitcast(F32), ALU.subtract), S("ya_ready1"), i + 1)
                link.leave(p.iters)

            def branches(name, X):
                p, x = ph[name], name[-1]
                dve.wait_ge(S(f"gates_ready{x}"), HEADS)
                with dve.Fori(0, p.iters) as i:
                    link.enter(i, 8 * 2)
                    for b in range(p.blocks):
                        low_part(p, i, b)
                        j, half = divmod(b, 2)
                        tile_sum(p, i, b, b, b, acc[half], wk(half))
                        gate = G[:, ds(i * 16 + (4 * (j // 2) + 2 * half + j % 2), 1), :]
                        link(V.tensor_tensor(work[:, half:half + 1, 0:T], work[:, half:half + 1, 0:T], gate, ALU.mult))
                        if half:
                            mark(V.tensor_tensor(wk(0), wk(0), wk(1), ALU.add), S(f"mz_ready{x}"), i * 8 + j + 1)
                            dve.wait_ge(S(f"mh_ready{x}"), i * 8 + j + 1)
                            mark(V.tensor_tensor(X[:, ds(i * 8 + j, 1), T:2 * T], work[:, 0:1, 0:T],
                                                 X[:, ds(i * 8 + j, 1), 0:T].bitcast(F32), ALU.subtract),
                                 S(f"m_ready{x}"), i * 8 + j + 1)
                    link.leave(p.iters)

            def add_to_residual(p, i, b, t, bank, j):
                dve.wait_ge(w_used, p.block(i, b) + 1)
                h = hT[:, ds(j, 1), :]
                link(V.tensor_tensor(h, bank[:, 0:T].rearrange("p (a t) -> p a t", a=1), h, ALU.add))
                mark(V.tensor_tensor(h, bank[:, T:2 * T].rearrange("p (a t) -> p a t", a=1), h, ALU.add), acc_free,
                     p.tile(i, t) + 1 + TILE_CREDIT)

            def low_operand(n, X, j, wcol):
                dve.wait_ge(uh_ready, n + 1)
                mark(V.scalar_tensor_tensor(X[:, ds(j, 1), T:2 * T], hT[:, ds(j, 1), :], wcol,
                                            X[:, ds(j, 1), 0:T].bitcast(F32), ALU.mult, ALU.subtract), x_ready, n + 1)

            def out_projection(name, X, n0, c0):
                p = ph[name]
                with dve.Fori(0, p.iters) as i:
                    link.enter(i, 8)
                    for b in range(p.blocks):
                        low_part(p, i, b)
                        if b % 2:
                            j = i * 8 + b // 2
                            add_to_residual(p, i, b, b // 2, acc[b // 2 % 2], j)
                            low_operand(n0 * KD + j, X, j, cols[:, ds(j + c0, 1)])
                    link.leave(p.iters)

            branches("branch1", XU)
            out_projection("out1", XY, 1, C_MLP1)
            dve.wait_ge(rs_ready, 2)

            def ffn1(p, i, n, last):
                for b in range(p.blocks):
                    low_part(p, i, b)
                    if b < 2 * KB and b % 2:
                        t = b // 2
                        tile_sum(p, i, t, b, t, acc[t % 2], wk(0))
                        link(V.tensor_tensor(wk(0), wk(0), rs[:, :], ALU.mult))
                        mark(V.scalar_tensor_tensor(wk(1), wk(0), 0.0, wk(0), ALU.max, ALU.mult), S("act1_z"), n * KB + t + 1)
                        dve.wait_ge(S("act1_hi"), n * KB + t + 1)
                        mark(V.tensor_tensor(XU[:, t, T:2 * T], wk(1), XU[:, t, 0:T].bitcast(F32), ALU.subtract),
                             S("act1_ready"), n * KB + t + 1)
                    if b >= 2 * KB:
                        j = b - 2 * KB
                        add_to_residual(p, i, b, KB + j, acc[b % 2], j)
                        if last:
                            low_operand(2 * KD + j, XY, j, fm2[:, j:j + 1])

            with dve.Fori(0, ph["ffn1"].iters) as i:
                link.enter(i, 8 + 16)
                ffn1(ph["ffn1"], i, i, False)
                link.leave(ph["ffn1"].iters)
            ffn1(ph["ffn1last"], 0, ph["ffn1"].iters, True)

            dve.wait_ge(S("rs1_ready"), 1)
            dve.wait_ge(stat_done, 4)
            link(V.tensor_tensor(wk(8), psX[:, 0:T], rs1[:, :], ALU.mult))
            mark(V.tensor_tensor(wk(8), wk(8), rs1[:, :], ALU.mult), S("ms2_ready"), 1)
            dve.wait_ge(rs_ready, 3)
            link(V.tensor_tensor(rs[:, :], rs[:, :], rs1[:, :], ALU.mult))

            p = ph["gmv"]
            for b in range(p.blocks):
                low_part(p, 0, b)
                t = b // 2
                link(V.scalar_tensor_tensor(hT[:, b, :], hT[:, b, :], cols[:, C_FIN1 + b:C_FIN1 + b + 1], rs1[:, :], ALU.mult, ALU.mult))
                if b % 2:
                    if t == 0:
                        dve.wait_ge(S("wsT_full"), 1)
                    scaled_tile(p, 0, t, b, t, acc[t % 2], G[:, 24 + t, :], S("gv_z"), t + 1)
            dve.wait_ge(S("gv_sum"), 1)
            link(V.tensor_scalar(wk(8), psT[:, 0:T], 1.0 / WIDTH, None, ALU.mult))
            for t in range(HEADS):
                link(V.tensor_tensor(G[:, 24 + t, :], G[:, 24 + t, :], wk(8), ALU.subtract))
                if t >= 2:
                    dve.wait_ge(S("gv_sq_used"), t - 1)
                mark(V.tensor_tensor(wk(t % 2), G[:, 24 + t, :], G[:, 24 + t, :], ALU.mult), S("gv_sq"), t + 1)
            dve.wait_ge(S("gv_rstd"), 1)
            dve.wait_ge(S("bs_in"), 32)
            dve.wait_ge(S("wsT_ready"), 2)

            p = ph["heads2"]
            with dve.Fori(0, p.iters) as i:
                link.enter(i, PER_HEADS2)
                for b in range(p.blocks):
                    low_part(p, i, b)
                    t = b // 2
                    bank = acc[t % 2]
                    if b == 0:
                        link(V.tensor_tensor(work[:, 3:4, 0:T], G[:, ds(i + 24, 1), :], rs1[:, :].rearrange("p (a t) -> p a t", a=1), ALU.mult))
                        mark(V.tensor_scalar(wk(3), wk(3), cols[:, ds(i + C_LNG, 1)], cols[:, ds(i + C_LNB, 1)], ALU.mult, ALU.add),
                             S("vh_ready"), i + 1)
                    if b == 1:
                        scaled_tile(p, i, 0, b, 0, bank, wk(0), S("u_z"), i + 1)
                    if b == 3:
                        scaled_tile(p, i, 1, b, 1, bank, wk(7), S("k_z2"), i + 1)
                    if b == 5:
                        scaled_tile(p, i, 2, b, 2, bank, wk(6), S("qk_ready2"), i + 1)
                    if b == 6:
                        dve.wait_ge(S("mix_full"), i + 1)
                        bs = HS[:, 2:4, :, :].rearrange("p a b c -> p (a b) c")[:, ds(i, 1), :].to_broadcast([P, NT, P])
                        link(V.tensor_tensor(wk(1).rearrange("p (a t) -> p a t", a=NT), psA[:, 0:T].rearrange("p (a t) -> p a t", a=NT),
                                             bs, ALU.add))
                        dve.wait_ge(S("u_ready"), i + 1)
                        mark(V.tensor_tensor(wk(1), wk(1), wk(0), ALU.mult), S("ya_z2"), i + 1)
                        dve.wait_ge(S("yah_ready2"), i + 1)
                        mark(V.tensor_tensor(XU[:, ds(i, 1), T:2 * T], work[:, 1:2, 0:T],
                                             XU[:, ds(i, 1), 0:T].bitcast(F32), ALU.subtract), S("ya_ready2"), i + 1)
                        dve.wait_ge(S("bias2_in"), 64 * i + 64)
                        for h in range(2):
                            part = bias[:, h, :].rearrange("p (j k) -> p j k", k=64)
                            link(V.tensor_tensor(part, part, kTop[:, 0:64].rearrange("p (a k) -> p a k", a=1).to_broadcast([P, 6, 64]), ALU.add))
                    if b == 7:
                        scaled_tile(p, i, 3, b, 3, bank, wk(5), S("avz_ready2"), i + 1)
                        softmax_front(0, T, 2, i)
                    if b == 8:
                        softmax_back(0, T, 2, i)
                    if b == 9:
                        tile_sum(p, i, 4, b, 4, bank, wk(8))
                        link(V.tensor_tensor(G[:, ds(i * 4, 1), :], work[:, 8:9, 0:T], rs[:, :].rearrange("p (a t) -> p a t", a=1), ALU.mult))
                        softmax_front(1, T, 2, i)
                    if b == 10:
                        softmax_back(1, T, 2, i)
                    if b in (11, 13, 15):
                        n = (b - 9) // 2
                        tile_sum(p, i, 4 + n, b, 4 + n, bank, wk(8))
                        ins = V.tensor_tensor(G[:, ds(i * 4 + n, 1), :], work[:, 8:9, 0:T],
                                              rs[:, :].rearrange("p (a t) -> p a t", a=1), ALU.mult)
                        if n == 3:
                            mark(ins, S("gates_z2"), i + 1)
                        else:
                            link(ins)
                    if b == 14:
                        low_of_attention(2, i, XU)
                link.leave(p.iters)

            branches("branch2", XY)
            out_projection("out2", XU, 3, C_FFN2)
            for val in range(2):
                for edge in (0, T + 1):
                    link(V.memset(work[:, val, edge:edge + 1], 0.0))
            dve.wait_ge(rs_ready, 4)

            def ffn2(p, i, n, f0, last):
                nk = FF2 % KB if p.name == "ffn2tail" else KB
                for b in range(p.blocks):
                    low_part(p, i, b)
                    if b < 4 * nk and b % 2:
                        t, val = divmod(b // 2, 2)
                        z = work[:, val, 1:T + 1]
                        tile_sum(p, i, b // 2, b, b // 2, acc[b // 2 % 2], z)
                        mark(V.tensor_tensor(z, z, rs[:, :], ALU.mult), S("conv_z"), (n + t) * 2 + val + 1)
                        ch = f0 + t + val * FF2
                        c = wk(2 + val)
                        dve.wait_ge(S("conv_first"), (n + t) * 2 + val + 1)
                        link(V.scalar_tensor_tensor(c, z, convc[:, 1, ds(ch, 1)], c, ALU.mult, ALU.add))
                        ins = V.scalar_tensor_tensor(c, work[:, val, 2:T + 2], convc[:, 2, ds(ch, 1)], c, ALU.mult, ALU.add)
                        if val == 0:
                            mark(ins, S("gate_conv"), n + t + 1)
                        else:
                            link(ins)
                            dve.wait_ge(S("gate_silu"), n + t + 1)
                            mark(V.tensor_tensor(wk(5), wk(4), c, ALU.mult), S("act2_z"), n + t + 1)
                            dve.wait_ge(S("act2_hi"), n + t + 1)
                            mark(V.tensor_tensor(XY[:, t, T:2 * T], wk(5), XY[:, t, 0:T].bitcast(F32), ALU.subtract),
                                 S("act2_ready"), n + t + 1)
                    if b >= 4 * nk:
                        if p.name == "ffn2tail":
                            for c in range(2):
                                j = 2 * (b - 4 * nk) + c
                                add_to_residual(p, i, b, 2 * nk + j, acc[j % 2], j)
                        else:
                            j = b - 4 * nk
                            add_to_residual(p, i, b, 2 * nk + j, acc[j % 2], j)
                            if last and j >= 2:
                                copy_out(j - 2)

            def copy_out(j):
                dve.wait_ge(S("outT_full"), j + 1)
                o = Gf[:, 0:NT * D].rearrange("p (a n) -> p a n", a=NT)[:, :, j * P:(j + 1) * P]
                mark(V.tensor_copy(o, (psE, psA)[j % 2][:, 0:T].rearrange("p (a n) -> p a n", a=NT)), S("out_copied"), j + 1)

            ffn2(ph["ffn2tail"], 0, 0, 0, False)
            with dve.Fori(0, ph["ffn2"].iters) as i:
                link.enter(i, 8 * 3 + 16)
                ffn2(ph["ffn2"], i, i * KB + FF2 % KB, i * KB + FF2 % KB, False)
                link.leave(ph["ffn2"].iters)
            ffn2(ph["ffn2last"], 0, FF2 - KB, FF2 - KB, True)
            copy_out(KD - 2)
            copy_out(KD - 1)
            dve.wait_ge(S("out_rstd"), 1)
            for c in range(2):
                part = Gf[:, c * D // 2:(c + 1) * D // 2]
                V.tensor_scalar(part, part, small[:, 6:7], None, ALU.mult).then_inc(S("out_scaled0"), 1)


PER_HEADS1 = 21
PER_HEADS2 = 15


def shape_constants():
    t = np.arange(P)
    s_, t_ = t[:, None], t[None, :]
    sums = np.zeros((9, P, P), np.float32)
    masks = np.zeros((9, P, P), np.float32)
    sums[0] = s_ > t_
    sums[8] = s_ <= t_
    masks[0] = masks[8] = np.eye(P)
    for l in range(7):
        z = 1 << l
        mid = t_ // (2 * z) * (2 * z) + z
        upper = t_ % (2 * z) >= z
        sums[l + 1] = np.where(upper, (s_ >= mid) & (s_ <= t_), (s_ > t_) & (s_ < mid))
        masks[l + 1] = (s_ // (2 * z) == t_ // (2 * z)) & (s_ % (2 * z) < z) & upper
    c = np.arange(64)
    start = np.clip(c - 8, 0, 48)
    inside = (c[None, :] >= start[:, None]) & (c[None, :] < start[:, None] + 16)
    window = np.where(inside, 0.0, MASKED).astype(np.float32)[:, ::-1]
    flat = lambda m: np.ascontiguousarray(m.transpose(1, 0, 2).reshape(P, 9 * P))
    return {"range_sums": flat(sums), "pair_masks": flat(masks), "identity": np.eye(P, dtype=np.float32),
            "window": np.concatenate([window, window])}


_INS = ["x", "w_in", "lb_logits", "hg_norm_w", "rel_bias", "w_branch_a", "w_branch_b", "w_out", "norm_mix_w",
        "norm_mlp_w", "w_up", "w_down", "norm_final_w", "norm_mix_2", "w_in_2", "gm_ln_g_2", "gm_ln_b_2",
        "gm_w_s_2", "gm_b_s_2", "na_rpb_2", "w_branch_2", "w_out_2", "norm_ffn_2", "w_up_2", "conv_k_2",
        "conv_b_2", "w_down_2", "norm_final_2"]


def kernel(**inputs):
    import concourse.bacc as bacc
    from concourse.bass_utils import run_bass_kernel_spmd

    nc = bacc.Bacc("TRN2", target_bir_lowering=False, num_devices=1, dynamic_dma_scratch_size=1024)
    arrays = {f"in_{n}": np.ascontiguousarray(inputs[n]) for n in _INS}
    arrays |= {f"in_{n}": a for n, a in shape_constants().items()}
    args = [nc.dram_tensor(n, a.shape, F32, kind="ExternalInput").ap() for n, a in arrays.items()]
    args.append(nc.dram_tensor("out_dram", (1, T, D), F32, kind="ExternalOutput").ap())
    two_blocks(nc, *args)
    r = run_bass_kernel_spmd(nc, [arrays], core_ids=[0])
    return r.results[0]["out_dram"]
```

```python
from contextlib import ExitStack

import concourse.bass as bass
import numpy as np
from concourse import mybir

F32 = mybir.dt.float32
F32R = mybir.dt.float32r
BF16 = mybir.dt.bfloat16
ALU = mybir.AluOpType
ACT = mybir.ActivationFunctionType
AX_X = mybir.AxisListType.X
ds = bass.ds

P = 128
T = 256
NT = T // P
D = 2048
KD = D // P
HEADS = 8
WIDTH = HEADS * P
FF1 = 4 * D // P
FF2 = 5504 // P
N_REL = 513
RPB_R, RPB_C = 15, 31
AT_SCALE = 64 ** -0.5
HG_SCALE = P ** -0.5
MASKED = -3.0e38
RMS_EPS = 1e-6
LN_EPS = 1e-5
NREL_COLS = 384
RPB_BACK = RPB_R * RPB_C - 1 - (10 * RPB_C + 63 + 15)

SLOTS = 5
REUSE = 4
LEAD = 4
KB = 8
BLOCK = KB * P


class Phase:

    def __init__(self, name, before, iters, blocks, tiles, crosses, shapes=None):
        self.name, self.iters, self.blocks, self.tiles, self.crosses = name, iters, blocks, tiles, crosses
        fives = next(n for n in range(blocks) if (blocks - 5 * n) % 4 == 0)
        self.slots = [s for n in [5] * fives + [4] * ((blocks - 5 * fives) // 4) for s in range(n)]
        self.uses = [self.slots.count(s) for s in range(SLOTS)]
        if before is None:
            self.base, self.tbase, self.cbase, self.used = 0, 0, 0, [0] * SLOTS
        else:
            self.base = before.base + before.iters * before.blocks
            self.tbase = before.tbase + before.iters * before.tiles
            self.cbase = before.cbase + before.iters * before.crosses
            self.used = [u + before.iters * n for u, n in zip(before.used, before.uses)]
        self.shapes = shapes or {}

    def block(self, i, b):
        return self.base + self.blocks * i + b

    def tile(self, i, t):
        return self.tbase + self.tiles * i + t

    def cross(self, i, c):
        return self.cbase + self.crosses * i + c

    def slot(self, b):
        return self.slots[b] if b < self.blocks else b - self.blocks

    def landed(self, i, b):
        s = self.slot(b)
        if b < self.blocks:
            return (self.used[s] + self.slots[:b].count(s) + 1) * 16 + self.uses[s] * 16 * i
        return (self.used[s] + self.uses[s] + 1) * 16 + self.uses[s] * 16 * i

    def size(self, b):
        kt, cols = self.shapes.get(b, (KB, P))
        return kt * cols


class Step:

    def __init__(self, kind, group, t, value=0, half=0):
        self.kind, self.group, self.t, self.value, self.half = kind, group, t, value, half


def up_steps(group, t, values):
    return [Step("up", group, t, value, half) for value in range(values) for half in range(2)]


def mixed_steps(group, values, down):
    share = len(down) // KB
    return [s for t in range(KB) for s in up_steps(group, t, values) + down[t * share:(t + 1) * share]]


def ffn_steps():
    def downs(group):
        return [Step("down", group, j) for j in range(KD)]

    tail = [Step("down", -1, j) for j in range(0, KD, 2)]
    return {
        "ffn1first": [s for t in range(KB) for s in up_steps(0, t, 1)] + mixed_steps(1, 1, downs(0)),
        "ffn1": mixed_steps(2, 1, downs(1)) + mixed_steps(3, 1, downs(2)),
        "ffn1last": downs(FF1 // KB - 1),
        "ffn2first": [s for t in range(FF2 % KB) for s in up_steps(-1, t, 2)] + mixed_steps(0, 2, tail),
        "ffn2": mixed_steps(1, 2, downs(0)) + mixed_steps(2, 2, downs(1)),
        "ffn2last": downs(FF2 // KB - 1),
    }


FFN = ffn_steps()


def ffn_counts(name):
    ups = sum(s.kind == "up" and s.half == 1 for s in FFN[name])
    downs = sum((2 if s.group < 0 else 1) for s in FFN[name] if s.kind == "down")
    return len(FFN[name]), ups + downs, ups


def phases():
    tail = {b: (FF2 % KB, 2 * P) for b, s in enumerate(FFN["ffn2first"]) if s.kind == "down"}
    plan = [("heads1", HEADS, 22, 11, 11, None), ("branch1", 2, 16, 16, 16, None), ("out1", 2, 16, 8, 0, None),
            ("ffn1first", 1, *ffn_counts("ffn1first"), None),
            ("ffn1", FF1 // KB // 2 - 1, *ffn_counts("ffn1"), None),
            ("ffn1last", 1, *ffn_counts("ffn1last"), None),
            ("gmv", 1, 16, 8, 8, None), ("heads2", HEADS, 16, 8, 8, None),
            ("branch2", 2, 16, 16, 16, None), ("out2", 2, 16, 8, 0, None),
            ("ffn2first", 1, *ffn_counts("ffn2first"), tail),
            ("ffn2", FF2 // KB // 2, *ffn_counts("ffn2"), None),
            ("ffn2last", 1, *ffn_counts("ffn2last"), None)]
    out, before = {}, None
    for name, iters, blocks, tiles, crosses, shapes in plan:
        before = out[name] = Phase(name, before, iters, blocks, tiles, crosses, shapes)
    return out


class Link:

    def __init__(self, eng, sem):
        self.eng, self.sem, self.base, self.k, self.i, self.per = eng, sem, 0, 0, None, 0

    def __call__(self, ins):
        self.k += 1
        ins.then_inc(self.sem, 1)
        at = self.base + self.k
        self.eng.wait_ge(self.sem, at if self.i is None else self.i * self.per + at)

    def enter(self, i, per):
        self.base, self.k, self.i, self.per = self.base + self.k, 0, i, per

    def leave(self, n):
        assert self.k == self.per, (self.k, self.per)
        self.base, self.k, self.i = self.base + n * self.per, 0, None


def two_blocks(
    nc, x, w_in, lb_logits, hg_norm_w, rel_bias, w_branch_a, w_branch_b, w_out, norm_mix_w, norm_mlp_w,
    w_up, w_down, norm_final_w, norm_mix_2, w_in_2, gm_ln_g_2, gm_ln_b_2, gm_w_s_2, gm_b_s_2, na_rpb_2,
    w_branch_2, w_out_2, norm_ffn_2, w_up_2, conv_k_2, conv_b_2, w_down_2, norm_final_2,
    range_sums, pair_masks, identity, window, out,
):
    ph = phases()
    last_phase = ph["ffn2last"]

    with ExitStack() as ctx:
        def sb(name, shape, dt=F32):
            return ctx.enter_context(nc.sbuf_tensor(name, shape, dt))

        def psum(name):
            return ctx.enter_context(nc.psum_tensor(name, [P, 512], F32))

        def sem(name):
            return ctx.enter_context(nc.semaphore(name))

        w_raw = [sb(f"w_raw{s}", [P, BLOCK]) for s in range(SLOTS)]
        w_hi = [sb(f"w_hi{s}", [P, BLOCK], F32R) for s in range(SLOTS)]
        w_lo = [sb(f"w_lo{s}", [P, BLOCK], F32R) for s in range(SLOTS)]
        hT = sb("hT", [P, KD, T])
        XU = sb("XU", [P, KD, 2 * T], F32R)
        XY = sb("XY", [P, KD, 2 * T], F32R)
        G = sb("G", [P, 2 * KD, T])
        Gf = G[:, :, :].rearrange("p a t -> p (a t)")
        sums = sb("sums", [P, 9, P], F32R)
        masks = sb("masks", [P, 9, P], BF16)
        ident = sb("ident", [P, P])
        ones = sb("ones", [P, P])
        cols = sb("cols", [P, P])
        convc = sb("convc", [P, 4, 2 * FF2])
        small = sb("small", [P, 64])
        HS = sb("HS", [P, 4, 4, P])
        work = sb("work", [P, 9, T + 2])
        cross = sb("cross", [P, 2, T])
        rs = sb("rs", [P, T])
        rs1 = sb("rs1", [P, T])
        sqacc = sb("sqacc", [P, 2, T])
        sqb = sb("sqb", [P, 2, T])
        lg_hi = sb("lg_hi", [P, NT, P], F32R)
        lg_lo = sb("lg_lo", [P, NT, P], F32R)
        AT = sb("AT", [P, 3, P])
        kTop = sb("kTop", [P, P])
        v_nat = sb("v_nat", [P, NT, P])
        av_nat = sb("av_nat", [P, NT, P])
        probs = sb("probs", [P, NT, 2, T])
        pT = sb("pT", [P, 4, P])
        bias = sb("bias", [P, 2, NREL_COLS])
        soft = sb("soft", [P, 4, 2, 2])

        acc = [psum("acc0"), psum("acc1")]
        acc_first = psum("acc_first")
        psE, psA, psT, psS, psX = (psum(n) for n in ("psE", "psA", "psT", "psS", "psX"))

        rpb_back = nc.dram_tensor("rpb_back", (2 * HEADS, RPB_R * RPB_C), F32, kind="Internal").ap()

        C_MIX1, C_MLP1, C_FIN1, C_MIX2, C_FFN2, C_FIN2, C_LB, C_LNG, C_LNB = 0, 16, 32, 48, 64, 80, 96, 112, 120
        eps_rms, eps_ln, hgw = small[:, 0:1], small[:, 1:2], small[:, 2:3]
        lbc, omlb, fm2 = small[:, 8:16], small[:, 16:24], small[:, 24:40]
        lbt = small[:, 40:64]

        def wk(n):
            return work[:, n, 0:T]

        four_banks = [acc[0], acc[1], psT, psX]

        def ffn_bank(name, t):
            shift = -ffn_counts(name)[1] % 4 if name.endswith("first") else 0
            return four_banks[(t + shift) % 4]

        def complete(step):
            return step.kind == "up" and step.half == 1

        def gate_of(i, b):
            j, half = divmod(b, 2)
            return i * 16 + (4 * (j // 2) + 2 * half + j % 2)

        def mixed_before(b, blocks):
            return [b // 2 - 1] if b and b % 2 == 0 else [b // 2] if b == blocks - 1 else []

        def made(name, i, group):
            if group < 0:
                return 0
            return (i * 2 + group) * KB + (0 if name.startswith("ffn1") else FF2 % KB)

        def ring_half(group, n):
            return group % 2 * KB + n

        landed = [sem(f"landed{s}") for s in range(SLOTS)]
        hi_done, lo_dve, lo_pool, w_used = sem("hi_done"), sem("lo_dve"), sem("lo_pool"), sem("w_used")
        acc_free, cross_ready = sem("acc_free"), sem("cross_ready")
        dve_step, act_step = sem("dve_step"), sem("act_step")
        x_in, c_in, v_in = sem("x_in"), sem("c_in"), sem("v_in")
        h_ready, sq_ready, sq_added, uh_ready, x_ready = (
            sem(n) for n in ("h_ready", "sq_ready", "sq_added", "uh_ready", "x_ready"))
        sq2_ready, sq2_added = sem("sq2_ready"), sem("sq2_added")
        stat_done, rs_ready = sem("stat_done"), sem("rs_ready")
        names = {}

        def S(name):
            if name not in names:
                names[name] = sem(name)
            return names[name]

        CREDIT = REUSE
        TILE_CREDIT = 2

        block = ctx.enter_context(nc.Block())

        def weight_source(name, i, b):
            def part(w, row, ntiles, col, ncols=P):
                n = w.shape[1]
                return w.tensor, row * n + col, [[n, P], [P * n, ntiles], [1, ncols]]

            half = b % 2
            if name == "heads1":
                t = b // 2
                starts = [0, 1, 3, 2, 5, 4, 6]
                col = starts[t] * WIDTH + i * P if t < 7 else (7 * WIDTH + (t - 7) // 2 * D + (t - 7) % 2 * P + i * (2 * P))
                return part(w_in[0], half * BLOCK, KB, col)
            if name == "heads2":
                t = b // 2
                starts = [0, 3, 2, 4]
                col = starts[t] * WIDTH + i * P if t < 4 else (5 * WIDTH + (t - 4) // 2 * D + (t - 4) % 2 * P + i * (2 * P))
                return part(w_in_2[0], half * BLOCK, KB, col)
            if name == "gmv":
                return part(w_in_2[0], half * BLOCK, KB, WIDTH + b // 2 * P)
            if name == "branch1":
                return part((w_branch_a, w_branch_b)[half][0], 0, KB, i * (8 * P) + b // 2 * P)
            if name == "branch2":
                return part(w_branch_2[0], half * BLOCK, KB, i * (8 * P) + b // 2 * P)
            if name in ("out1", "out2"):
                return part((w_out if name == "out1" else w_out_2)[0], half * BLOCK, KB, i * (8 * P) + b // 2 * P)
            step = FFN[name][b]
            if name.startswith("ffn1"):
                first = (i * 2 + step.group) * BLOCK
                if step.kind == "up":
                    return part(w_up[0], step.half * BLOCK, KB, first + step.t * P)
                return part(w_down[0], first, KB, step.t * P)
            first = 0 if step.group < 0 else (FF2 % KB) * P + (i * 2 + step.group) * BLOCK
            if step.kind == "up":
                return part(w_up_2[0], step.half * BLOCK, KB, first + (step.t + step.value * FF2) * P)
            if step.group < 0:
                return part(w_down_2[0], 0, FF2 % KB, step.t * P, 2 * P)
            return part(w_down_2[0], first, KB, step.t * P)

        @block.sync
        def _(sp):
            def load(name, p, i, b):
                kt, ncols = p.shapes.get(b, (KB, P))
                s = p.slot(b)
                tensor, offset, ap = weight_source(name, i, b)
                freed = p.block(i, b) - REUSE + 1 + CREDIT
                sp.wait_ge(lo_dve, freed)
                sp.wait_ge(lo_pool, freed)
                sp.dma_start(w_raw[s][:, 0:kt * ncols].rearrange("p (k n) -> p k n", k=kt),
                             bass.AP(tensor=tensor, offset=offset, ap=ap)).then_inc(landed[s], 16)

            xn = Gf[:, 0:NT * D].rearrange("p (a n) -> p a n", a=NT)
            for a in range(NT):
                sp.dma_start(xn[:, a, :], x[0, a * P:(a + 1) * P, :]).then_inc(x_in, 16)

            def side(name, i, b):
                if name == "heads1" and b == 6:
                    offset = sp.snap(i * (2 * N_REL) + 1)
                    sp.wait_ge(S("scores_read1"), i * 2)
                    sp.dma_start(bias[:, :, :], bass.AP(tensor=rel_bias.tensor, offset=offset,
                                                        ap=[[1, P], [N_REL, 2], [1, NREL_COLS]])).then_inc(S("bias1_in"), 16)
                if name == "ffn1last" and b == 0:
                    sp.dma_start(Gf[:, 0:WIDTH].rearrange("p (g q) -> p g q", g=HEADS),
                                 gm_w_s_2[0].rearrange("g p q -> p g q")).then_inc(S("ws_in"), 16)
                    sp.dma_start(HS[:, 2:4, :, :].rearrange("p a b c -> p (a b c)"),
                                 bass.AP(tensor=gm_b_s_2.tensor, offset=0, ap=[[0, P], [1, WIDTH]])).then_inc(S("bs_in"), 16)
                    sp.dma_start(kTop[:, 0:64], window).then_inc(S("bs_in"), 16)
                if name == "gmv" and b == 0:
                    sp.wait_ge(S("rpb_out"), 16)
                if name == "heads2" and b == 6:
                    offset = sp.snap(i * (2 * RPB_R * RPB_C) + RPB_BACK)
                    sp.wait_ge(S("scores_read2"), i * 2)
                    for r in range(2):
                        for h in range(2):
                            sp.dma_start(
                                bias[64 * r:64 * r + 64, h, :].rearrange("p (j k) -> p j k", k=64),
                                bass.AP(tensor=rpb_back.tensor,
                                        offset=offset + (h * RPB_R * RPB_C + r * RPB_C),
                                        ap=[[1, 64], [RPB_C, 6], [1, 64]])).then_inc(S("bias2_in"), 16)

            for name, p in ph.items():
                if p.iters == 1:
                    for b in range(p.blocks):
                        load(name, p, 0, b)
                        side(name, 0, b)
                else:
                    with sp.Fori(0, p.iters) as i:
                        for b in range(p.blocks):
                            load(name, p, i, b)
                            side(name, i, b)
            sp.wait_ge(S("out_done"), 16 * 2 * NT)

        @block.tensor
        def _(pe):
            def products(p, i, b, bank, X, k0, first, last, nk=KB, col=0, width=P, operand=None):
                s = p.slot(b)
                hi = w_hi[s][:, 0:nk * width].rearrange("p (k n) -> p k n", k=nk)
                lo = w_lo[s][:, 0:nk * width].rearrange("p (k n) -> p k n", k=nk)
                if col == 0:
                    pe.wait_ge(lo_dve, p.block(i, b) + 1 + CREDIT)
                    pe.wait_ge(lo_pool, p.block(i, b) + 1 + CREDIT)
                for k in range(nk):
                    if operand is not None:
                        pe.wait_ge(operand[0], operand[1] + k0 + k + 1)
                    nc.tensor.matmul(bank[:, :], hi[:, k, col:col + P], X[:, k0 + k, :],
                                     start=first and k == 0, stop=False, skip_group_check=True)
                    done = nc.tensor.matmul(bank[:, 0:T], lo[:, k, col:col + P], X[:, k0 + k, 0:T],
                                            start=False, stop=last and k == nk - 1, skip_group_check=True)
                if col + P == width:
                    done.then_inc(w_used, 1)

            def bank_free(p, i, t):
                pe.wait_ge(acc_free, p.tile(i, t) - 1 + TILE_CREDIT)

            def rms_sum(source=0, dst=psS):
                nc.tensor.matmul(dst[:, 0:T], ones[:, :], sqacc[:, source, :], start=True, stop=True).then_inc(stat_done, 1)

            pe.wait_ge(c_in, 16)
            pe.wait_ge(x_in, 16 * NT)
            xn = Gf[:, 0:NT * D].rearrange("p (a n) -> p a n", a=NT)
            banks = [psE, psA]
            for j in range(0, KD, 2):
                n = j // 2
                if n >= 2:
                    pe.wait_ge(h_ready, 2 * n - 2)
                for jj in range(2):
                    for a in range(NT):
                        done = nc.tensor.transpose(banks[n % 2][:, (jj * NT + a) * P:(jj * NT + a + 1) * P],
                                                   xn[:, a, (j + jj) * P:(j + jj + 1) * P], ident[:, :])
                done.then_inc(S("xt_full"), 1)
                if n == 1:
                    pe.wait_ge(v_in, 16 * 9)
                    nc.tensor.transpose(psT[:, 0:P], Gf[:, 4096:4096 + P], ident[:, :]).then_inc(S("vec_full"), 1)
            pe.wait_ge(S("conv_in"), 32)
            for t in range(4):
                done = nc.tensor.transpose(psX[:, t * 2 * FF2:(t + 1) * 2 * FF2],
                                           Gf[0:2 * FF2, 4224 + t * P:4224 + (t + 1) * P], ident[0:2 * FF2, 0:2 * FF2])
            done.then_inc(S("conv_full"), 1)
            pe.wait_ge(sq_added, KD)
            rms_sum()

            p = ph["heads1"]

            def in_tiles(p, i, X, after, bank_of):
                for b in range(p.blocks):
                    t = b // 2
                    if b % 2 == 0:
                        bank_free(p, i, t)
                    products(p, i, b, bank_of(t), X, KB * (b % 2), b % 2 == 0, b % 2 == 1)
                    for job in after.get(b, []):
                        job(i)

            def transpose_pair(src, wait_name, full_name, read=None):
                def job(i):
                    if read is not None:
                        pe.wait_ge(S(read), i + 1)
                    pe.wait_ge(S(wait_name), i + 1)
                    for a in range(NT):
                        done = nc.tensor.transpose(psT[:, a * P:(a + 1) * P], src[:, a * P:(a + 1) * P], ident[:, :])
                    done.then_inc(S(full_name), 1)
                return job

            def decays(k):
                a, h = divmod(k, 2)
                def job(i):
                    if k == 0:
                        pe.wait_ge(S("lg_lo_ready"), i + 1)
                    else:
                        pe.wait_ge(S("decay_exp"), i * 4 + k)
                    rhs = sums[:, 4 * h + a:4 * h + a + 4, :]
                    nc.tensor.matmul(psE[:, :], lg_hi[:, a, :], rhs, start=True, stop=False)
                    nc.tensor.matmul(psE[:, :], lg_lo[:, a, :], rhs, start=False, stop=True).then_inc(S("decay_full"), 1)
                return job

            def pair_products(k):
                a, h = divmod(k, 2)
                def job(i):
                    pe.wait_ge(S("qE_ready"), i * 4 + k + 1)
                    pe.wait_ge(S("kE_ready"), i * 4 + k + 1)
                    if k:
                        pe.wait_ge(S("psA_read"), i * 4 + k)
                    for l in range(4):
                        if (k, l) in ((0, 0), (3, 3)):
                            lhsT, rhs = wk(1)[:, a * P:(a + 1) * P], wk(2)[:, a * P:(a + 1) * P]
                        else:
                            lhsT, rhs = HS[:, 2, l, :], HS[:, 1, l, :]
                        done = nc.tensor.matmul(psA[:, l * P:(l + 1) * P], lhsT, rhs, start=True, stop=True)
                    done.then_inc(S("pairs_full"), 1)
                return job

            def tile_pairs(i):
                pe.wait_ge(S("psA_read"), i * 4 + 4)
                nc.tensor.matmul(psA[:, 0:P], kTop[:, :], HS[:, 1, 3, :], start=True, stop=True).then_inc(S("top_full"), 1)

            def scan_out(i):
                pe.wait_ge(S("AT_ready"), i + 1)
                pe.wait_ge(S("top_copied"), i + 1)
                pe.wait_ge(S("v_ready"), i + 1)
                nc.tensor.matmul(psE[:, 0:T], v_nat[:, 0, :], AT[:, 0:2, :], start=True, stop=False, skip_group_check=True)
                nc.tensor.matmul(psE[:, P:T], v_nat[:, 1, :], AT[:, 2, :], start=False, stop=True,
                                 skip_group_check=True).then_inc(S("o_full"), 1)

            def scan_rms(i):
                pe.wait_ge(S("o_sq"), i + 1)
                nc.tensor.matmul(psE[:, 0:T], ones[:, :], wk(4), start=True, stop=True).then_inc(S("o_sum"), 1)

            def scores(a, nk, x):
                def job(i):
                    if a == 0:
                        pe.wait_ge(S(f"qk_ready{x}"), i + 1)
                        pe.wait_ge(S(f"yb_ready{x}"), i)
                    else:
                        pe.wait_ge(S(f"scores_read{x}"), i * 2 + 1)
                    for h, bank in enumerate((psS, psX)):
                        q0 = 64 * h
                        done = nc.tensor.matmul(bank[:, 0:nk], wk(6)[q0:q0 + 64, a * P:(a + 1) * P],
                                                wk(7)[q0:q0 + 64, 0:nk], start=True, stop=True)
                    done.then_inc(S(f"scores_full{x}"), 1)
                return job

            def prob_transposes(h, x):
                parts = [(0, 0), (0, 1), (1, 1)] if x == 1 else [(0, 0), (0, 1), (1, 0), (1, 1)]
                def job(i):
                    pe.wait_ge(S(f"probs_ready{x}"), i * 2 + 2)
                    pe.wait_ge(S(f"av_ready{x}") if h == 0 else S(f"pT_ready{x}"), i + 1 if h == 0 else i * 2 + 1)
                    for n, (k, q) in enumerate(parts):
                        done = nc.tensor.transpose(psT[:, n * P:(n + 1) * P], probs[:, q, h, k * P:(k + 1) * P], ident[:, :])
                    done.then_inc(S(f"pT_full{x}"), 1)
                return job

            def attend(h, x):
                def job(i):
                    pe.wait_ge(S(f"pT_ready{x}"), i * 2 + h + 1)
                    dst = psS[64 * h:64 * h + 64, :]
                    nc.tensor.matmul(dst[:, 0:T], av_nat[:, 0, 64 * h:64 * h + 64], pT[:, 0:2, :],
                                     start=True, stop=False, skip_group_check=True)
                    if x == 1:
                        done = nc.tensor.matmul(dst[:, P:T], av_nat[:, 1, 64 * h:64 * h + 64], pT[:, 2, :],
                                                start=False, stop=True, skip_group_check=True)
                    else:
                        done = nc.tensor.matmul(dst[:, 0:T], av_nat[:, 1, 64 * h:64 * h + 64], pT[:, 2:4, :],
                                                start=False, stop=True, skip_group_check=True)
                    done.then_inc(S(f"attended{x}"), 1)
                return job

            after1 = {
                7: [transpose_pair(wk(0), "lg_ready", "lgT_full")],
                8: [decays(0)],
                9: [transpose_pair(wk(5), "vi_ready", "vT_full")],
                10: [pair_products(0), decays(1)],
                12: [pair_products(1), decays(2)],
                13: [scores(0, P, 1)],
                14: [pair_products(2), decays(3), transpose_pair(wk(5), "avz_ready", "avT_full", "v_ready")],
                15: [scores(1, T, 1)],
                16: [pair_products(3)],
                18: [tile_pairs],
                19: [scan_out, prob_transposes(0, 1)],
                20: [attend(0, 1), prob_transposes(1, 1)],
                21: [scan_rms, attend(1, 1)],
            }
            pe.wait_ge(x_ready, KD)
            with pe.Fori(0, p.iters) as i:
                in_tiles(p, i, XU, after1, lambda t: acc_first if t == 0 else acc[(t - 1) % 2])

            def branches(name):
                p = ph[name]
                X = XY if name == "branch1" else XU
                x = name[-1]
                with pe.Fori(0, p.iters) as i:
                    for b in range(p.blocks):
                        pe.wait_ge(acc_free, p.tile(i, b) - 3 + TILE_CREDIT)
                        if b < 2:
                            pe.wait_ge(acc_free, p.tbase - 1 + b + TILE_CREDIT)
                        if b == 1:
                            pe.wait_ge(S(f"yb_ready{x}"), HEADS)
                        products(p, i, b, four_banks[b % 4], X, KB * (b % 2), True, True,
                                 operand=(S(f"ya_ready{x}"), 0) if b == 0 else None)

            def out_projection(name):
                p = ph[name]
                X = XU if name == "out1" else XY
                with pe.Fori(0, p.iters) as i:
                    for b in range(p.blocks):
                        if b % 2 == 0:
                            bank_free(p, i, b // 2)
                        products(p, i, b, acc[b // 2 % 2], X, KB * (b % 2), b % 2 == 0, b % 2 == 1,
                                 operand=(S(f"m_ready{name[-1]}"), 0) if b < 2 else None)

            branches("branch1")
            out_projection("out1")

            def ffn_bank_free(p, i, t):
                back = 1 if p.name.endswith("first") and t < 4 else 3
                pe.wait_ge(acc_free, p.tile(i, t) - back + TILE_CREDIT)

            def ffn(name, i, X, A, ready, finish=None, operand=None, sums=0):
                p, tile, waited = ph[name], 0, set()
                for b, s in enumerate(FFN[name]):
                    if s.kind == "up":
                        if s.half == 0:
                            ffn_bank_free(p, i, tile)
                        products(p, i, b, ffn_bank(name, tile), X, KB * s.half, s.half == 0, s.half == 1,
                                 operand=operand if b < 2 else None)
                        if sums and b == 1:
                            pe.wait_ge(sq_added, sums)
                            rms_sum()
                        tile += s.half
                        continue
                    nk = FF2 % KB if s.group < 0 else KB
                    if s.group not in waited:
                        pe.wait_ge(ready, made(name, i, s.group) + nk)
                        waited.add(s.group)
                    for c in range(2 if s.group < 0 else 1):
                        ffn_bank_free(p, i, tile)
                        products(p, i, b, ffn_bank(name, tile), A, ring_half(s.group, 0), True, True, nk,
                                 c * P, 2 * P if s.group < 0 else P)
                        tile += 1
                    if finish is not None and s.t >= 2:
                        finish(s.t - 2)

            ffn("ffn1first", 0, XY, XU, S("act1_ready"), operand=(x_ready, KD), sums=2 * KD)
            with pe.Fori(0, ph["ffn1"].iters) as i:
                ffn("ffn1", i, XY, XU, S("act1_ready"))
            ffn("ffn1last", 0, XY, XU, S("act1_ready"))

            p = ph["gmv"]
            for b in range(p.blocks):
                if b % 2 == 0:
                    bank_free(p, 0, b // 2)
                products(p, 0, b, acc[b // 2 % 2], XY, KB * (b % 2), b % 2 == 0, b % 2 == 1,
                         operand=(x_ready, 2 * KD) if b < 2 else None)
                if b == 0:
                    pe.wait_ge(S("ws_in"), 16)
                    for g in range(HEADS):
                        bank = (psE, psA)[g // 4]
                        done = nc.tensor.transpose(bank[:, g % 4 * P:(g % 4 + 1) * P], Gf[:, g * P:(g + 1) * P], ident[:, :])
                    done.then_inc(S("wsT_full"), 1)
                if b == 1:
                    pe.wait_ge(sq_added, 3 * KD)
                    rms_sum()
                    pe.wait_ge(sq2_added, KD)
                    rms_sum(1, psX)
            pe.wait_ge(S("wsT_ready"), 2)
            for t in range(HEADS):
                pe.wait_ge(S("gv_ready"), t + 1)
                done = nc.tensor.matmul(psT[:, 0:T], ones[:, :], G[:, 24 + t, :], start=t == 0, stop=t == HEADS - 1)
            done.then_inc(S("gv_sum"), 1)
            for t in range(HEADS):
                pe.wait_ge(S("gv_sq"), t + 1)
                done = nc.tensor.matmul(psE[:, 0:T], ones[:, :], wk(t % 2), start=t == 0, stop=t == HEADS - 1)
                done.then_inc(S("gv_sq_used"), 1)

            def mix(i):
                pe.wait_ge(S("vn_ready"), i + 1)
                for n in range(NT):
                    done = nc.tensor.matmul(psA[:, n * P:(n + 1) * P], v_nat[:, n, :],
                                            HS[:, 0:2, :, :].rearrange("p a b c -> p (a b c)")[:, ds(i * P, P)],
                                            start=True, stop=True)
                done.then_inc(S("mix_full"), 1)

            after2 = {
                4: [transpose_pair(wk(3), "vh_ready", "vh_full")],
                6: [mix],
                7: [scores(0, T, 2)],
                8: [transpose_pair(wk(5), "avz_ready2", "avT_full2")],
                9: [scores(1, T, 2)],
                13: [prob_transposes(0, 2)],
                14: [attend(0, 2), prob_transposes(1, 2)],
                15: [attend(1, 2)],
            }
            p = ph["heads2"]
            with pe.Fori(0, p.iters) as i:
                in_tiles(p, i, XY, after2, lambda t: acc[t % 2])
            branches("branch2")
            out_projection("out2")
            def output_transposes(j):
                pe.wait_ge(S("hw_ready"), j + 1)
                bank = (psE, psA)[j % 2]
                if j >= 2:
                    pe.wait_ge(S("out_copied"), j - 1)
                for a in range(NT):
                    done = nc.tensor.transpose(bank[:, a * P:(a + 1) * P], sqb[:, j % 2, a * P:(a + 1) * P], ident[:, :])
                done.then_inc(S("outT_full"), 1)

            ffn("ffn2first", 0, XU, XY, S("act2_ready"), operand=(x_ready, 3 * KD), sums=4 * KD)
            with pe.Fori(0, ph["ffn2"].iters) as i:
                ffn("ffn2", i, XU, XY, S("act2_ready"))
            ffn("ffn2last", 0, XU, XY, S("act2_ready"), output_transposes)
            output_transposes(KD - 2)
            output_transposes(KD - 1)
            pe.wait_ge(S("sqf_added"), KD)
            for a in range(NT):
                done = nc.tensor.matmul(psT[:, a:a + 1], sqacc[:, 0, a * P:(a + 1) * P], ones[:, 0:1], start=True, stop=True)
            done.then_inc(S("out_sum"), 1)

        @block.scalar
        def _(act):
            link = Link(act, act_step)
            act.dma_start(ident[:, :], identity).then_inc(c_in, 16)
            for n, v in enumerate((norm_mix_w, norm_mlp_w, norm_final_w, norm_mix_2, norm_ffn_2, norm_final_2)):
                src = v[0] if len(v.shape) == 2 else v
                act.dma_start(Gf[16 * n:16 * n + 16, 4096:4096 + P], src.rearrange("(j p) -> j p", p=P)).then_inc(v_in, 16)
            act.dma_start(Gf[96:112, 4096:4096 + P], lb_logits.rearrange("l (j p) -> (l j) p", p=P)).then_inc(v_in, 16)
            act.dma_start(Gf[112:120, 4096:4096 + P], gm_ln_g_2[0].rearrange("(j p) -> j p", p=P)).then_inc(v_in, 16)
            act.dma_start(Gf[120:128, 4096:4096 + P], gm_ln_b_2[0].rearrange("(j p) -> j p", p=P)).then_inc(v_in, 16)
            act.dma_start(Gf[0:2 * FF2, 4224:4224 + 3 * P].rearrange("j (t p) -> j t p", t=3),
                          conv_k_2[0].rearrange("t (j p) -> j t p", p=P)).then_inc(S("conv_in"), 16)
            act.dma_start(Gf[0:2 * FF2, 4224 + 3 * P:4224 + 4 * P], conv_b_2[0].rearrange("(j p) -> j p", p=P)).then_inc(S("conv_in"), 16)
            act.dma_start(hgw, hg_norm_w.rearrange("a p -> p a")).then_inc(S("hgw_in"), 16)
            act.dma_start(Gf[:, 4736:4736 + 9 * P], range_sums).then_inc(S("sums_in"), 16)
            act.dma_start(Gf[:, 5888:5888 + 9 * P], pair_masks).then_inc(S("masks_in"), 16)

            rpb_in = Gf[0:2 * HEADS, 7040:7040 + RPB_R * RPB_C]
            rpb_turned = Gf[0:2 * HEADS, 7552:7552 + RPB_R * RPB_C]
            act.dma_start(rpb_in, na_rpb_2[0].rearrange("h r c -> h (r c)")).then_inc(S("rpb_in"), 16)

            def round_block(p, i, b):
                c = b + LEAD
                if p is last_phase and c >= p.blocks:
                    return
                s, n = p.slot(c), (p.size(c) if c < p.blocks else BLOCK)
                act.wait_ge(landed[s], p.landed(i, c))
                act.wait_ge(w_used, p.block(i, b) + 1)
                act.activation(w_hi[s][:, 0:n], w_raw[s][:, 0:n], ACT.Copy).then_inc(hi_done, 1)

            def copy_cross(p, i, c, b, bank):
                act.wait_ge(w_used, p.block(i, b) + 1)
                act.activation(cross[:, c % 2, :], bank[:, T:2 * T], ACT.Copy).then_inc(cross_ready, 1)

            def rstd(dst, src, width, eps, tmp, done):
                link(act.activation(tmp, src, ACT.Ln, bias=eps, scale=1.0 / width))
                act.activation(dst, tmp, ACT.Exp, scale=-0.5).then_inc(done, 1)

            act.wait_ge(lo_dve, CREDIT)
            for b in range(LEAD):
                act.wait_ge(landed[b], 16)
                act.activation(w_hi[b][:, :], w_raw[b][:, :], ACT.Copy).then_inc(hi_done, 1)
            for j in range(KD):
                act.wait_ge(h_ready, j + 1)
                if j == 0:
                    act.wait_ge(S("cols_ready"), 1)
                if j >= 2:
                    act.wait_ge(sq_added, j - 1)
                act.activation(sqb[:, j % 2, :], hT[:, j, :], ACT.Square).then_inc(sq_ready, 1)
                act.activation(XU[:, j, 0:T], hT[:, j, :], ACT.Copy, scale=cols[:, C_MIX1 + j:C_MIX1 + j + 1]).then_inc(uh_ready, 1)
            act.wait_ge(stat_done, 1)
            rstd(rs[:, :], psS[:, 0:T], D, eps_rms, rs1[:, :], rs_ready)
            act.wait_ge(S("lb_max"), 1)
            act.activation(lbt[:, 0:16], lbt[:, 0:16], ACT.Exp).then_inc(S("lb_exp"), 1)
            act.wait_ge(S("sums_in"), 16)
            link(act.activation(sums[:, :, :].rearrange("p a b -> p (a b)"), Gf[:, 4736:4736 + 9 * P], ACT.Copy))
            act.wait_ge(S("masks_in"), 16)
            link(act.activation(masks[:, :, :].rearrange("p a b -> p (a b)"), Gf[:, 5888:5888 + 9 * P], ACT.Copy))
            act.wait_ge(S("rpb_in"), 16)
            act.activation(rpb_turned, Gf[0:2 * HEADS, 7040 + RPB_R * RPB_C - 1:7039:-1], ACT.Copy).then_inc(S("rpb_turned"), 1)
            act.wait_ge(S("rpb_turned"), 1)
            act.dma_start(rpb_back, rpb_turned).then_inc(S("rpb_out"), 16)

            def sigmoid_of(n, wait_name, done_name, i):
                act.wait_ge(S(wait_name), i + 1)
                act.activation(wk(4), wk(n), ACT.Sigmoid).then_inc(S(done_name), 1)

            def softmax_exp(a, nk, x, i):
                act.wait_ge(S(f"max_ready{x}"), i * 2 + a + 1)
                for h in range(2):
                    ins = act.activation(probs[:, a, h, 0:nk], probs[:, a, h, 0:nk], ACT.Exp,
                                         bias=soft[:, 1, a, h:h + 1], accum_out=soft[:, 2, a, h:h + 1])
                    ins.then_inc(S(f"exp_done{x}"), 1)

            def evac_pT(h, x, i):
                n = 3 if x == 1 else 4
                act.wait_ge(S(f"pT_full{x}"), i * 2 + h + 1)
                if h == 1:
                    act.wait_ge(S(f"attended{x}"), i * 2 + 1)
                act.activation(pT[:, 0:n, :], psT[:, 0:n * P], ACT.Copy).then_inc(S(f"pT_ready{x}"), 1)

            def high_of_attention(x, i, X):
                act.wait_ge(S(f"attended{x}"), i * 2 + 2)
                act.activation(X[:, ds(i + HEADS, 1), 0:T], psS[:, 0:T].rearrange("p (a t) -> p a t", a=1),
                               ACT.Copy).then_inc(S(f"ybh_ready{x}"), 1)

            p = ph["heads1"]
            with act.Fori(0, p.iters) as i:
                link.enter(i, 1)
                for b in range(p.blocks):
                    round_block(p, i, b)
                    t = b // 2
                    if b % 2:
                        copy_cross(p, i, t, b, acc_first if t == 0 else acc[(t - 1) % 2])
                    if b == 1:
                        sigmoid_of(2, "hq_z", "hq_sig", i)
                    if b == 3:
                        act.wait_ge(S("q_ready"), i + 1)
                        sigmoid_of(0, "hf_z", "hf_sig", i)
                    if b == 5:
                        act.wait_ge(S("g_ready"), i + 1)
                        sigmoid_of(3, "hg_z", "hg_sig", i)
                        act.activation(wk(0), wk(0), ACT.Ln).then_inc(S("lg_ready"), 1)
                    if b == 7:
                        act.wait_ge(S("lgT_full"), i + 1)
                        act.activation(lg_hi[:, :, :], psT[:, 0:T], ACT.Copy).then_inc(S("lg_hi_ready"), 1)
                    if b in (8, 10, 12, 14):
                        k = (b - 8) // 2
                        act.wait_ge(S("decay_full"), i * 4 + k + 1)
                        if k:
                            act.wait_ge(S("qE_ready"), i * 4 + k)
                            act.wait_ge(S("kE_ready"), i * 4 + k)
                        act.activation(HS[:, 0, :, :], psE[:, :], ACT.Exp).then_inc(S("decay_exp"), 1)
                    if b == 9:
                        act.wait_ge(S("vT_full"), i + 1)
                        act.activation(v_nat[:, :, :], psT[:, 0:T], ACT.Copy).then_inc(S("v_ready"), 1)
                    if b == 14:
                        act.wait_ge(S("avT_full"), i + 1)
                        act.activation(av_nat[:, :, :], psT[:, 0:T], ACT.Copy).then_inc(S("av_ready1"), 1)
                    if b == 13:
                        softmax_exp(0, P, 1, i)
                    if b == 15:
                        softmax_exp(1, T, 1, i)
                    if b == 18:
                        act.wait_ge(S("top_full"), i + 1)
                        act.activation(AT[:, 1, :], psA[:, 0:P], ACT.Copy).then_inc(S("top_copied"), 1)
                    if b == 19:
                        act.wait_ge(S("o_full"), i + 1)
                        act.activation(wk(0), psE[:, 0:T], ACT.Copy).then_inc(S("o_copied"), 1)
                        evac_pT(0, 1, i)
                    if b == 20:
                        evac_pT(1, 1, i)
                    if b == 21:
                        act.wait_ge(S("o_sum"), i + 1)
                        link(act.activation(wk(5), psE[:, 0:T], ACT.Ln, bias=eps_rms, scale=1.0 / P))
                        act.activation(wk(5), wk(5), ACT.Exp, scale=-0.5).then_inc(S("o_rstd"), 1)
                        act.wait_ge(S("ya_z1"), i + 1)
                        act.activation(XY[:, ds(i, 1), 0:T], work[:, 0:1, 0:T], ACT.Copy).then_inc(S("yah_ready1"), 1)
                        high_of_attention(1, i, XY)
                link.leave(p.iters)

            def free_cross(p, i, t):
                act.wait_ge(acc_free, p.tile(i, t) - 1 + TILE_CREDIT)

            def branches(name, X):
                p, x = ph[name], name[-1]
                act.wait_ge(S(f"gates_z{x}"), HEADS)
                with act.Fori(0, p.iters) as i:
                    for b in range(p.blocks):
                        round_block(p, i, b)
                        gate = G[:, ds(gate_of(i, b), 1), :]
                        act.activation(gate, gate, ACT.Sigmoid).then_inc(S(f"gates_ready{x}"), 1)
                        free_cross(p, i, b)
                        copy_cross(p, i, b, b, four_banks[b % 4])
                        for j in mixed_before(b, p.blocks):
                            act.wait_ge(S(f"mz_ready{x}"), i * 8 + j + 1)
                            act.activation(X[:, ds(i * 8 + j, 1), 0:T], work[:, 2 * (j % 2):2 * (j % 2) + 1, 0:T], ACT.Copy)\
                               .then_inc(S(f"mh_ready{x}"), 1)

            def operand_tile(n, X, j, wcol, p, i, t):
                act.wait_ge(acc_free, p.tile(i, t) + 1 + TILE_CREDIT)
                act.wait_ge(sq_added, n)
                act.activation(sqb[:, 0:1, :], hT[:, ds(j, 1), :], ACT.Square).then_inc(sq_ready, 1)
                act.activation(X[:, ds(j, 1), 0:T], hT[:, ds(j, 1), :], ACT.Copy, scale=wcol).then_inc(uh_ready, 1)

            def out_projection(name, X, n0, c0):
                p = ph[name]
                with act.Fori(0, p.iters) as i:
                    for b in range(p.blocks):
                        round_block(p, i, b)
                        if b % 2:
                            j = i * 8 + b // 2
                            operand_tile(n0 * KD + j, X, j, cols[:, ds(j + c0, 1)], p, i, b // 2)

            branches("branch1", XU)
            out_projection("out1", XY, 1, C_MLP1)
            act.wait_ge(stat_done, 2)
            rstd(rs[:, :], psS[:, 0:T], D, eps_rms, rs1[:, :], rs_ready)

            def next_operand(p, j):
                operand_tile(2 * KD + j, XY, j, fm2[:, j:j + 1], p, 0, j)
                if j:
                    act.wait_ge(sq2_added, j)
                act.activation(sqb[:, 1, :], hT[:, j, :], ACT.Square,
                               scale=cols[:, C_FIN1 + j:C_FIN1 + j + 1]).then_inc(sq2_ready, 1)

            def ffn1(name, i):
                p, tile, c = ph[name], 0, 0
                for b, s in enumerate(FFN[name]):
                    round_block(p, i, b)
                    if s.kind == "up" and s.half:
                        free_cross(p, i, tile)
                        copy_cross(p, i, c, b, ffn_bank(name, tile))
                        n = made(name, i, s.group) + s.t
                        act.wait_ge(S("act1_z"), n + 1)
                        act.activation(XU[:, ring_half(s.group, s.t), 0:T], wk(1), ACT.Copy).then_inc(S("act1_hi"), 1)
                        c += 1
                    if name == "ffn1last" and b:
                        next_operand(p, b - 1)
                    tile += s.half if s.kind == "up" else 1

            ffn1("ffn1first", 0)
            with act.Fori(0, ph["ffn1"].iters) as i:
                ffn1("ffn1", i)
            ffn1("ffn1last", 0)
            next_operand(ph["ffn1last"], KD - 1)

            act.wait_ge(stat_done, 3)
            link(act.activation(rs[:, :], psS[:, 0:T], ACT.Ln, bias=eps_rms, scale=1.0 / D))
            act.activation(rs1[:, :], rs[:, :], ACT.Exp, scale=-0.5).then_inc(S("rs1_ready"), 1)
            act.wait_ge(S("ms2_ready"), 1)
            link(act.activation(rs[:, :], wk(8), ACT.Ln, bias=eps_rms, scale=1.0 / D))
            act.activation(rs[:, :], rs[:, :], ACT.Exp, scale=-0.5).then_inc(rs_ready, 1)
            act.wait_ge(S("wsT_full"), 1)
            for g, bank in enumerate((psE, psA)):
                act.activation(HS[:, g, :, :], bank[:, :], ACT.Copy).then_inc(S("wsT_ready"), 1)

            p = ph["gmv"]
            for b in range(p.blocks):
                round_block(p, 0, b)
                if b % 2:
                    t = b // 2
                    copy_cross(p, 0, t, b, acc[t % 2])
                    act.wait_ge(S("gv_z"), t + 1)
                    act.activation(G[:, 24 + t, :], G[:, 24 + t, :], ACT.Gelu_apprx_tanh).then_inc(S("gv_ready"), 1)
            act.wait_ge(S("gv_sq_used"), HEADS)
            rstd(rs1[:, :], psE[:, 0:T], WIDTH, eps_ln, wk(4), S("gv_rstd"))

            p = ph["heads2"]
            with act.Fori(0, p.iters) as i:
                for b in range(p.blocks):
                    round_block(p, i, b)
                    t = b // 2
                    if b % 2:
                        copy_cross(p, i, t, b, acc[t % 2])
                    if b == 1:
                        act.wait_ge(S("u_z"), i + 1)
                        act.activation(wk(0), wk(0), ACT.Gelu_apprx_tanh).then_inc(S("u_ready"), 1)
                    if b == 4:
                        act.wait_ge(S("vh_full"), i + 1)
                        act.activation(v_nat[:, :, :], psT[:, 0:T], ACT.Copy).then_inc(S("vn_ready"), 1)
                    if b == 6:
                        act.wait_ge(S("ya_z2"), i + 1)
                        act.activation(XU[:, ds(i, 1), 0:T], work[:, 1:2, 0:T], ACT.Copy).then_inc(S("yah_ready2"), 1)
                    if b == 8:
                        act.wait_ge(S("avT_full2"), i + 1)
                        act.activation(av_nat[:, :, :], psT[:, 0:T], ACT.Copy).then_inc(S("av_ready2"), 1)
                    if b == 7:
                        softmax_exp(0, T, 2, i)
                    if b == 9:
                        softmax_exp(1, T, 2, i)
                    if b == 13:
                        evac_pT(0, 2, i)
                    if b == 14:
                        evac_pT(1, 2, i)
                    if b == 15:
                        high_of_attention(2, i, XU)

            branches("branch2", XY)
            out_projection("out2", XU, 3, C_FFN2)
            act.wait_ge(stat_done, 5)
            rstd(rs[:, :], psS[:, 0:T], D, eps_rms, rs1[:, :], rs_ready)

            def final_tile(p, j):
                act.wait_ge(acc_free, p.tile(0, j) + 1 + TILE_CREDIT)
                if j >= 2:
                    act.wait_ge(S("outT_full"), j - 1)
                act.activation(sqb[:, j % 2, :], hT[:, j, :], ACT.Copy,
                               scale=cols[:, C_FIN2 + j:C_FIN2 + j + 1]).then_inc(S("hw_ready"), 1)
                if j >= 2:
                    act.wait_ge(S("sqf_added"), j - 1)
                act.activation(wk(6 + j % 2), hT[:, j, :], ACT.Square).then_inc(S("sqf_ready"), 1)

            def ffn2(name, i):
                p, tile, c = ph[name], 0, 0
                for b, s in enumerate(FFN[name]):
                    round_block(p, i, b)
                    if b and complete(FFN[name][b - 1]):
                        u = FFN[name][b - 1]
                        n = made(name, i, u.group) + u.t
                        act.wait_ge(S("conv_z"), n * 2 + u.value + 1)
                        ch = n + u.value * FF2
                        act.activation(wk(2 + u.value), work[:, u.value, 0:T], ACT.Identity, scale=convc[:, 0, ds(ch, 1)],
                                       bias=convc[:, 3, ds(ch, 1)]).then_inc(S("conv_first"), 1)
                        if u.value == 0:
                            act.wait_ge(S("gate_conv"), n + 1)
                            act.activation(wk(4), wk(2), ACT.Silu).then_inc(S("gate_silu"), 1)
                        else:
                            act.wait_ge(S("act2_z"), n + 1)
                            act.activation(XY[:, ring_half(u.group, u.t), 0:T], wk(5), ACT.Copy).then_inc(S("act2_hi"), 1)
                    if complete(s):
                        free_cross(p, i, tile)
                        copy_cross(p, i, c, b, ffn_bank(name, tile))
                        c += 1
                    if name == "ffn2last" and b:
                        final_tile(p, b - 1)
                    tile += s.half if s.kind == "up" else (2 if s.group < 0 else 1)

            ffn2("ffn2first", 0)
            with act.Fori(0, ph["ffn2"].iters) as i:
                ffn2("ffn2", i)
            ffn2("ffn2last", 0)
            final_tile(ph["ffn2last"], KD - 1)

            act.wait_ge(S("out_sum"), 1)
            link(act.activation(small[:, 4:6], psT[:, 0:NT], ACT.Ln, bias=eps_rms, scale=1.0 / D))
            act.activation(small[:, 6:8], small[:, 4:6], ACT.Exp, scale=-0.5).then_inc(S("out_rstd"), 1)
            act.wait_ge(S("out_rstd"), 1)
            act.wait_ge(S("out_copied"), KD)
            for c in range(2):
                part = Gf[:, D + c * D // 2:D + (c + 1) * D // 2]
                act.activation(part, part, ACT.Copy, scale=small[:, 7:8]).then_inc(S("out_scaled1"), 1)
                act.wait_ge(S("out_scaled1"), c + 1)
                act.dma_start(out[0, P:2 * P, c * D // 2:(c + 1) * D // 2], part).then_inc(S("out_done"), 16)
            for c in range(2):
                act.wait_ge(S("out_scaled0"), c + 1)
                act.dma_start(out[0, 0:P, c * D // 2:(c + 1) * D // 2], Gf[:, c * D // 2:(c + 1) * D // 2])\
                   .then_inc(S("out_done"), 16)

        @block.gpsimd
        def _(pool):
            def low_part(p, i, b):
                c = b + LEAD
                if p is last_phase and c >= p.blocks:
                    return
                s, n = p.slot(c), (p.size(c) if c < p.blocks else BLOCK)
                pool.wait_ge(hi_done, p.block(i, c) + 1)
                nc.gpsimd.tensor_tensor(w_lo[s][:, n // 2:n], w_raw[s][:, n // 2:n], w_hi[s][:, n // 2:n].bitcast(F32),
                                        ALU.subtract).then_inc(lo_pool, 1)

            def add_square(n):
                pool.wait_ge(sq_ready, n + 1)
                nc.gpsimd.tensor_tensor(sqacc[:, 0, :], sqacc[:, 0, :], sqb[:, 0, :], ALU.add).then_inc(sq_added, 1)
                pool.wait_ge(sq_added, n + 1)

            def clear_sums():
                nc.gpsimd.memset(sqacc[:, :, :], 0.0).then_inc(S("sums_cleared"), 1)
                cleared[0] += 1
                pool.wait_ge(S("sums_cleared"), cleared[0])

            cleared = [0]
            for n in range(CREDIT):
                nc.gpsimd.memset(ones[:, n * 32:(n + 1) * 32], 1.0).then_inc(lo_pool, 1)
            clear_sums()
            for b in range(LEAD):
                pool.wait_ge(hi_done, b + 1)
                nc.gpsimd.tensor_tensor(w_lo[b][:, BLOCK // 2:], w_raw[b][:, BLOCK // 2:], w_hi[b][:, BLOCK // 2:].bitcast(F32),
                                        ALU.subtract).then_inc(lo_pool, 1)
            for j in range(KD):
                pool.wait_ge(sq_ready, j + 1)
                nc.gpsimd.tensor_tensor(sqacc[:, 0, :], sqacc[:, 0, :], sqb[:, j % 2, :], ALU.add).then_inc(sq_added, 1)
                pool.wait_ge(sq_added, j + 1)

            p = ph["heads1"]
            with pool.Fori(0, p.iters) as i:
                for b in range(p.blocks):
                    low_part(p, i, b)
                    if b in (8, 10, 12, 14):
                        k = (b - 8) // 2
                        pool.wait_ge(S("decay_exp"), i * 4 + k + 1)
                        if k == 0:
                            pool.wait_ge(S("g_ready"), i + 1)
                        else:
                            pool.wait_ge(S("pairs_full"), i * 4 + k)
                        kk = wk(1)[:, (k // 2) * P:(k // 2 + 1) * P].rearrange("p (a t) -> p a t", a=1)
                        nc.gpsimd.tensor_tensor(HS[:, 2, :, :], HS[:, 0, :, :], kk.to_broadcast([P, 4, P]), ALU.mult)\
                          .then_inc(S("kE_ready"), 1)

            def plain(name):
                p = ph[name]
                if p.iters == 1:
                    for b in range(p.blocks):
                        low_part(p, 0, b)
                else:
                    with pool.Fori(0, p.iters) as i:
                        for b in range(p.blocks):
                            low_part(p, i, b)

            def out_projection(name, n0):
                p = ph[name]
                with pool.Fori(0, p.iters) as i:
                    for b in range(p.blocks):
                        low_part(p, i, b)
                        if b % 2:
                            add_square(i * 8 + (n0 * KD + b // 2))

            plain("branch1")
            pool.wait_ge(stat_done, 1)
            clear_sums()
            out_projection("out1", 1)
            plain("ffn1first")
            plain("ffn1")
            pool.wait_ge(stat_done, 2)
            clear_sums()
            p = ph["ffn1last"]
            for b in range(p.blocks):
                low_part(p, 0, b)
                add_square(2 * KD + b)
                pool.wait_ge(sq2_ready, b + 1)
                nc.gpsimd.tensor_tensor(sqacc[:, 1, :], sqacc[:, 1, :], sqb[:, 1, :], ALU.add).then_inc(sq2_added, 1)
                pool.wait_ge(sq2_added, b + 1)
            plain("gmv")
            plain("heads2")
            plain("branch2")
            pool.wait_ge(stat_done, 4)
            clear_sums()
            out_projection("out2", 3)
            plain("ffn2first")
            plain("ffn2")
            pool.wait_ge(stat_done, 5)
            clear_sums()
            p = ph["ffn2last"]
            for b in range(p.blocks):
                low_part(p, 0, b)
                pool.wait_ge(S("sqf_ready"), b + 1)
                nc.gpsimd.tensor_tensor(sqacc[:, 0, :], sqacc[:, 0, :], wk(6 + b % 2), ALU.add).then_inc(S("sqf_added"), 1)
                pool.wait_ge(S("sqf_added"), b + 1)

        @block.vector
        def _(dve):
            link = Link(dve, dve_step)
            V = nc.vector

            def mark(ins, s, value):
                ins.then_inc(s, 1)
                dve.wait_ge(s, value)

            def low_part(p, i, b):
                c = b + LEAD
                if p is last_phase and c >= p.blocks:
                    return
                s, n = p.slot(c), (p.size(c) if c < p.blocks else BLOCK)
                dve.wait_ge(hi_done, p.block(i, c) + 1)
                V.tensor_tensor(w_lo[s][:, 0:n // 2], w_raw[s][:, 0:n // 2], w_hi[s][:, 0:n // 2].bitcast(F32),
                                ALU.subtract).then_inc(lo_dve, 1)

            def tile_sum(p, i, c, b, t, bank, dst):
                dve.wait_ge(cross_ready, p.cross(i, c) + 1)
                mark(V.tensor_tensor(dst, bank[:, 0:T], cross[:, c % 2, :], ALU.add), acc_free,
                     p.tile(i, t) + 1 + TILE_CREDIT)

            def scaled_tile(p, i, c, b, t, bank, dst, s, value):
                tile_sum(p, i, c, b, t, bank, dst)
                mark(V.tensor_tensor(dst, dst, rs[:, :], ALU.mult), s, value)

            for n, (dst, value) in enumerate(((eps_rms, RMS_EPS), (eps_ln, LN_EPS), (small[:, 3:4], 0.0), (small[:, 4:5], 0.0))):
                V.memset(dst, value).then_inc(lo_dve, 1)
            for n in range(TILE_CREDIT):
                V.memset(small[:, 5 + n:6 + n], 0.0).then_inc(acc_free, 1)
            dve.wait_ge(lo_dve, CREDIT)
            dve.wait_ge(acc_free, TILE_CREDIT)
            for b in range(LEAD):
                dve.wait_ge(hi_done, b + 1)
                V.tensor_tensor(w_lo[b][:, 0:BLOCK // 2], w_raw[b][:, 0:BLOCK // 2], w_hi[b][:, 0:BLOCK // 2].bitcast(F32),
                                ALU.subtract).then_inc(lo_dve, 1)
            banks = (psE, psA)

            def first_low(j):
                dve.wait_ge(uh_ready, j + 1)
                V.scalar_tensor_tensor(XU[:, j, T:2 * T], hT[:, j, :], cols[:, C_MIX1 + j:C_MIX1 + j + 1],
                                       XU[:, j, 0:T].bitcast(F32), ALU.mult, ALU.subtract).then_inc(x_ready, 1)

            for j in range(0, KD, 2):
                dve.wait_ge(S("xt_full"), j // 2 + 1)
                V.tensor_copy(hT[:, j, :], banks[j // 2 % 2][:, 0:T]).then_inc(h_ready, 1)
                mark(V.tensor_copy(hT[:, j + 1, :], banks[j // 2 % 2][:, T:2 * T]), h_ready, j + 2)
                if j == 2:
                    dve.wait_ge(S("vec_full"), 1)
                    mark(V.tensor_copy(cols[:, :], psT[:, 0:P]), S("cols_ready"), 1)
                if j:
                    first_low(j - 2)
                    first_low(j - 1)
            first_low(KD - 2)
            first_low(KD - 1)
            link(V.tensor_tensor(lbt[:, 16:24], cols[:, C_LB:C_LB + 8], cols[:, C_LB + 8:C_LB + 16], ALU.max))
            link(V.tensor_tensor(lbt[:, 0:8], cols[:, C_LB:C_LB + 8], lbt[:, 16:24], ALU.subtract))
            mark(V.tensor_tensor(lbt[:, 8:16], cols[:, C_LB + 8:C_LB + 16], lbt[:, 16:24], ALU.subtract), S("lb_max"), 1)
            dve.wait_ge(S("lb_exp"), 1)
            link(V.tensor_tensor(lbt[:, 16:24], lbt[:, 0:8], lbt[:, 8:16], ALU.add))
            link(V.reciprocal(lbt[:, 16:24], lbt[:, 16:24]))
            link(V.tensor_tensor(lbc, lbt[:, 0:8], lbt[:, 16:24], ALU.mult))
            link(V.tensor_tensor(omlb, lbt[:, 8:16], lbt[:, 16:24], ALU.mult))
            link(V.tensor_tensor(fm2, cols[:, C_FIN1:C_FIN1 + KD], cols[:, C_MIX2:C_MIX2 + KD], ALU.mult))
            dve.wait_ge(S("conv_full"), 1)
            link(V.tensor_copy(convc[:, :, :], psX[:, 0:8 * FF2].rearrange("p (t j) -> p t j", t=4)))

            def softmax_front(a, nk, x, i):
                dve.wait_ge(S(f"scores_full{x}"), i * 2 + a + 1)
                for h, bank in enumerate((psS, psX)):
                    c1 = P * a + T - 1
                    rel = bias[:, h, c1:(c1 - nk if c1 >= nk else None):-1]
                    link(V.scalar_tensor_tensor(probs[:, a, h, 0:nk], bank[:, 0:nk], AT_SCALE, rel, ALU.mult, ALU.add))
                mark(V.reduce_max(soft[:, 0, a, :], probs[:, a, :, 0:nk], AX_X), S(f"scores_read{x}"), i * 2 + a + 1)
                mark(V.tensor_scalar(soft[:, 1, a, :], soft[:, 0, a, :], -1.0, None, ALU.mult), S(f"max_ready{x}"), i * 2 + a + 1)

            def softmax_back(a, nk, x, i):
                dve.wait_ge(S(f"exp_done{x}"), i * 4 + 2 * a + 2)
                link(V.reciprocal(soft[:, 3, a, :], soft[:, 2, a, :]))
                link(V.tensor_scalar(probs[:, a, 0, 0:nk], probs[:, a, 0, 0:nk], soft[:, 3, a, 0:1], None, ALU.mult))
                mark(V.tensor_scalar(probs[:, a, 1, 0:nk], probs[:, a, 1, 0:nk], soft[:, 3, a, 1:2], None, ALU.mult),
                     S(f"probs_ready{x}"), i * 2 + a + 1)

            def low_of_attention(x, i, X):
                dve.wait_ge(S(f"ybh_ready{x}"), i + 1)
                mark(V.tensor_tensor(X[:, ds(i + HEADS, 1), T:2 * T], psS[:, 0:T].rearrange("p (a t) -> p a t", a=1),
                                     X[:, ds(i + HEADS, 1), 0:T].bitcast(F32), ALU.subtract), S(f"yb_ready{x}"), i + 1)

            p = ph["heads1"]
            dve.wait_ge(rs_ready, 1)
            with dve.Fori(0, p.iters) as i:
                link.enter(i, PER_HEADS1)
                for b in range(p.blocks):
                    low_part(p, i, b)
                    t = b // 2
                    bank = acc_first if t == 0 else acc[(t - 1) % 2]
                    if b == 1:
                        scaled_tile(p, i, 0, b, 0, bank, wk(2), S("hq_z"), i + 1)
                    if b == 2:
                        dve.wait_ge(S("hq_sig"), i + 1)
                        mark(V.scalar_tensor_tensor(wk(2), wk(2), HG_SCALE, wk(4), ALU.mult, ALU.mult), S("q_ready"), i + 1)
                    if b == 3:
                        scaled_tile(p, i, 1, b, 1, bank, wk(0), S("hf_z"), i + 1)
                    if b == 4:
                        dve.wait_ge(S("hf_sig"), i + 1)
                        link(V.tensor_scalar(wk(0), wk(4), omlb[:, ds(i, 1)], lbc[:, ds(i, 1)], ALU.mult, ALU.add))
                        mark(V.tensor_scalar(wk(1), wk(0), -1.0, 1.0, ALU.mult, ALU.add), S("g_ready"), i + 1)
                    if b == 5:
                        scaled_tile(p, i, 2, b, 2, bank, wk(3), S("hg_z"), i + 1)
                    if b == 6:
                        dve.wait_ge(S("hg_sig"), i + 1)
                        link(V.scalar_tensor_tensor(wk(3), wk(3), hgw, wk(4), ALU.mult, ALU.mult))
                    if b == 7:
                        dve.wait_ge(S("lg_hi_ready"), i + 1)
                        mark(V.tensor_tensor(lg_lo[:, :, :], psT[:, 0:T].rearrange("p (a k) -> p a k", a=NT),
                                             lg_hi[:, :, :].bitcast(F32), ALU.subtract), S("lg_lo_ready"), i + 1)
                        scaled_tile(p, i, 3, b, 3, bank, wk(5), S("vi_ready"), i + 1)
                    if b == 8:
                        dve.wait_ge(S("bias1_in"), 16 * i + 16)
                        link(V.memset(bias[0:64, :, P:P + 64], MASKED))
                    if b in (8, 10, 12, 14):
                        k = (b - 8) // 2
                        dve.wait_ge(S("decay_exp"), i * 4 + k + 1)
                        if k:
                            dve.wait_ge(S("pairs_full"), i * 4 + k)
                        q = wk(2)[:, (k // 2) * P:(k // 2 + 1) * P].rearrange("p (a t) -> p a t", a=1)
                        if k == 0:
                            link(V.tensor_tensor(kTop[:, :], HS[:, 0, 0, :], wk(1)[:, 0:P], ALU.mult))
                        mark(V.tensor_tensor(HS[:, 1, :, :], HS[:, 0, :, :], q.to_broadcast([P, 4, P]), ALU.mult),
                             S("qE_ready"), i * 4 + k + 1)
                    if b == 9:
                        scaled_tile(p, i, 4, b, 4, bank, wk(7), S("k_z"), i + 1)
                    if b in (10, 12, 14, 16):
                        k = (b - 10) // 2
                        a, h = divmod(k, 2)
                        dve.wait_ge(S("pairs_full"), i * 4 + k + 1)
                        m0 = 4 * h + a
                        mark(V.tensor_tensor(HS[:, 3, :, :], psA[:, :].rearrange("p (l t) -> p l t", l=4),
                                             masks[:, m0:m0 + 4, :], ALU.mult), S("psA_read"), i * 4 + k + 1)
                        dst = AT[:, 2 * a, :] if h == 0 else wk(8)[:, 0:P]
                        link(V.tensor_reduce(dst, HS[:, 3, :, :].rearrange("p l t -> p t l"), AX_X, ALU.add))
                        if h:
                            ins = V.tensor_tensor(AT[:, 2 * a, :], AT[:, 2 * a, :], wk(8)[:, 0:P], ALU.add)
                            if a:
                                mark(ins, S("AT_ready"), i + 1)
                            else:
                                link(ins)
                    if b == 11:
                        scaled_tile(p, i, 5, b, 5, bank, wk(6), S("qk_ready1"), i + 1)
                    if b == 13:
                        scaled_tile(p, i, 6, b, 6, bank, wk(5), S("avz_ready"), i + 1)
                        softmax_front(0, P, 1, i)
                    if b == 14:
                        softmax_back(0, P, 1, i)
                    if b == 15:
                        dve.wait_ge(S("rpb_out"), 16)
                        tile_sum(p, i, 7, b, 7, bank, wk(8))
                        link(V.tensor_tensor(G[:, ds(i * 4, 1), :], work[:, 8:9, 0:T], rs[:, :].rearrange("p (a t) -> p a t", a=1), ALU.mult))
                        softmax_front(1, T, 1, i)
                    if b == 16:
                        softmax_back(1, T, 1, i)
                    if b in (17, 19, 21):
                        n = (b - 15) // 2
                        tile_sum(p, i, 7 + n, b, 7 + n, bank, wk(8))
                        ins = V.tensor_tensor(G[:, ds(i * 4 + n, 1), :], work[:, 8:9, 0:T],
                                              rs[:, :].rearrange("p (a t) -> p a t", a=1), ALU.mult)
                        if n == 3:
                            mark(ins, S("gates_z1"), i + 1)
                        else:
                            link(ins)
                    if b == 19:
                        dve.wait_ge(S("o_copied"), i + 1)
                        mark(V.tensor_tensor(wk(4), wk(0), wk(0), ALU.mult), S("o_sq"), i + 1)
                    if b == 21:
                        dve.wait_ge(S("o_rstd"), i + 1)
                        link(V.tensor_tensor(wk(0), wk(0), wk(5), ALU.mult))
                        mark(V.tensor_tensor(wk(0), wk(0), wk(3), ALU.mult), S("ya_z1"), i + 1)
                        dve.wait_ge(S("yah_ready1"), i + 1)
                        mark(V.tensor_tensor(XY[:, ds(i, 1), T:2 * T], work[:, 0:1, 0:T],
                                             XY[:, ds(i, 1), 0:T].bitcast(F32), ALU.subtract), S("ya_ready1"), i + 1)
                        low_of_attention(1, i, XY)
                link.leave(p.iters)

            def branches(name, X):
                p, x = ph[name], name[-1]
                with dve.Fori(0, p.iters) as i:
                    link.enter(i, 8 * 2)
                    for b in range(p.blocks):
                        low_part(p, i, b)
                        j, half = divmod(b, 2)
                        at = 2 * (j % 2)
                        z = work[:, at + half:at + half + 1, 0:T]
                        tile_sum(p, i, b, b, b, four_banks[b % 4], wk(at + half))
                        gate = G[:, ds(gate_of(i, b), 1), :]
                        dve.wait_ge(S(f"gates_ready{x}"), i * 16 + b + 1)
                        link(V.tensor_tensor(z, z, gate, ALU.mult))
                        if half:
                            mark(V.tensor_tensor(wk(at), wk(at), wk(at + 1), ALU.add), S(f"mz_ready{x}"), i * 8 + j + 1)
                        for j in mixed_before(b, p.blocks):
                            dve.wait_ge(S(f"mh_ready{x}"), i * 8 + j + 1)
                            mark(V.tensor_tensor(X[:, ds(i * 8 + j, 1), T:2 * T], work[:, 2 * (j % 2):2 * (j % 2) + 1, 0:T],
                                                 X[:, ds(i * 8 + j, 1), 0:T].bitcast(F32), ALU.subtract),
                                 S(f"m_ready{x}"), i * 8 + j + 1)
                    link.leave(p.iters)

            def add_to_residual(p, i, b, t, bank, j):
                dve.wait_ge(w_used, p.block(i, b) + 1)
                h = hT[:, ds(j, 1), :]
                link(V.tensor_tensor(h, bank[:, 0:T].rearrange("p (a t) -> p a t", a=1), h, ALU.add))
                mark(V.tensor_tensor(h, bank[:, T:2 * T].rearrange("p (a t) -> p a t", a=1), h, ALU.add), acc_free,
                     p.tile(i, t) + 1 + TILE_CREDIT)

            def low_operand(n, X, j, wcol):
                dve.wait_ge(uh_ready, n + 1)
                mark(V.scalar_tensor_tensor(X[:, ds(j, 1), T:2 * T], hT[:, ds(j, 1), :], wcol,
                                            X[:, ds(j, 1), 0:T].bitcast(F32), ALU.mult, ALU.subtract), x_ready, n + 1)

            def out_projection(name, X, n0, c0):
                p = ph[name]
                with dve.Fori(0, p.iters) as i:
                    link.enter(i, 8)
                    for b in range(p.blocks):
                        low_part(p, i, b)
                        if b % 2:
                            j = i * 8 + b // 2
                            add_to_residual(p, i, b, b // 2, acc[b // 2 % 2], j)
                            low_operand(n0 * KD + j, X, j, cols[:, ds(j + c0, 1)])
                    link.leave(p.iters)

            branches("branch1", XU)
            out_projection("out1", XY, 1, C_MLP1)
            dve.wait_ge(rs_ready, 2)

            def ffn1(name, i):
                p, tile, c = ph[name], 0, 0
                for b, s in enumerate(FFN[name]):
                    low_part(p, i, b)
                    bank = ffn_bank(name, tile)
                    if s.kind == "up" and s.half:
                        tile_sum(p, i, c, b, tile, bank, wk(0))
                        link(V.tensor_tensor(wk(0), wk(0), rs[:, :], ALU.mult))
                        n, at = made(name, i, s.group) + s.t, ring_half(s.group, s.t)
                        mark(V.scalar_tensor_tensor(wk(1), wk(0), 0.0, wk(0), ALU.max, ALU.mult), S("act1_z"), n + 1)
                        dve.wait_ge(S("act1_hi"), n + 1)
                        mark(V.tensor_tensor(XU[:, at, T:2 * T], wk(1), XU[:, at, 0:T].bitcast(F32), ALU.subtract),
                             S("act1_ready"), n + 1)
                        c += 1
                    if s.kind == "down":
                        add_to_residual(p, i, b, tile, bank, s.t)
                        if name == "ffn1last" and s.t:
                            low_operand(2 * KD + s.t - 1, XY, s.t - 1, fm2[:, s.t - 1:s.t])
                    tile += s.half if s.kind == "up" else 1

            ffn1("ffn1first", 0)
            with dve.Fori(0, ph["ffn1"].iters) as i:
                link.enter(i, 2 * (KB + KD))
                ffn1("ffn1", i)
                link.leave(ph["ffn1"].iters)
            ffn1("ffn1last", 0)
            low_operand(3 * KD - 1, XY, KD - 1, fm2[:, KD - 1:KD])

            dve.wait_ge(S("rs1_ready"), 1)
            dve.wait_ge(stat_done, 4)
            link(V.tensor_tensor(wk(8), psX[:, 0:T], rs1[:, :], ALU.mult))
            mark(V.tensor_tensor(wk(8), wk(8), rs1[:, :], ALU.mult), S("ms2_ready"), 1)
            dve.wait_ge(rs_ready, 3)
            link(V.tensor_tensor(rs[:, :], rs[:, :], rs1[:, :], ALU.mult))

            p = ph["gmv"]
            for b in range(p.blocks):
                low_part(p, 0, b)
                t = b // 2
                link(V.scalar_tensor_tensor(hT[:, b, :], hT[:, b, :], cols[:, C_FIN1 + b:C_FIN1 + b + 1], rs1[:, :], ALU.mult, ALU.mult))
                if b % 2:
                    if t == 0:
                        dve.wait_ge(S("wsT_full"), 1)
                    scaled_tile(p, 0, t, b, t, acc[t % 2], G[:, 24 + t, :], S("gv_z"), t + 1)
            dve.wait_ge(S("gv_sum"), 1)
            link(V.tensor_scalar(wk(8), psT[:, 0:T], 1.0 / WIDTH, None, ALU.mult))
            for t in range(HEADS):
                link(V.tensor_tensor(G[:, 24 + t, :], G[:, 24 + t, :], wk(8), ALU.subtract))
                if t >= 2:
                    dve.wait_ge(S("gv_sq_used"), t - 1)
                mark(V.tensor_tensor(wk(t % 2), G[:, 24 + t, :], G[:, 24 + t, :], ALU.mult), S("gv_sq"), t + 1)
            dve.wait_ge(S("gv_rstd"), 1)
            dve.wait_ge(S("bs_in"), 32)
            dve.wait_ge(S("wsT_ready"), 2)

            p = ph["heads2"]
            with dve.Fori(0, p.iters) as i:
                link.enter(i, PER_HEADS2)
                for b in range(p.blocks):
                    low_part(p, i, b)
                    t = b // 2
                    bank = acc[t % 2]
                    if b == 0:
                        link(V.tensor_tensor(work[:, 3:4, 0:T], G[:, ds(i + 24, 1), :], rs1[:, :].rearrange("p (a t) -> p a t", a=1), ALU.mult))
                        mark(V.tensor_scalar(wk(3), wk(3), cols[:, ds(i + C_LNG, 1)], cols[:, ds(i + C_LNB, 1)], ALU.mult, ALU.add),
                             S("vh_ready"), i + 1)
                    if b == 1:
                        scaled_tile(p, i, 0, b, 0, bank, wk(0), S("u_z"), i + 1)
                    if b == 3:
                        scaled_tile(p, i, 1, b, 1, bank, wk(7), S("k_z2"), i + 1)
                    if b == 5:
                        scaled_tile(p, i, 2, b, 2, bank, wk(6), S("qk_ready2"), i + 1)
                    if b == 6:
                        dve.wait_ge(S("mix_full"), i + 1)
                        bs = HS[:, 2:4, :, :].rearrange("p a b c -> p (a b) c")[:, ds(i, 1), :].to_broadcast([P, NT, P])
                        link(V.tensor_tensor(wk(1).rearrange("p (a t) -> p a t", a=NT), psA[:, 0:T].rearrange("p (a t) -> p a t", a=NT),
                                             bs, ALU.add))
                        dve.wait_ge(S("u_ready"), i + 1)
                        mark(V.tensor_tensor(wk(1), wk(1), wk(0), ALU.mult), S("ya_z2"), i + 1)
                        dve.wait_ge(S("yah_ready2"), i + 1)
                        mark(V.tensor_tensor(XU[:, ds(i, 1), T:2 * T], work[:, 1:2, 0:T],
                                             XU[:, ds(i, 1), 0:T].bitcast(F32), ALU.subtract), S("ya_ready2"), i + 1)
                        dve.wait_ge(S("bias2_in"), 64 * i + 64)
                        for h in range(2):
                            part = bias[:, h, :].rearrange("p (j k) -> p j k", k=64)
                            link(V.tensor_tensor(part, part, kTop[:, 0:64].rearrange("p (a k) -> p a k", a=1).to_broadcast([P, 6, 64]), ALU.add))
                    if b == 7:
                        scaled_tile(p, i, 3, b, 3, bank, wk(5), S("avz_ready2"), i + 1)
                        softmax_front(0, T, 2, i)
                    if b == 8:
                        softmax_back(0, T, 2, i)
                    if b == 9:
                        tile_sum(p, i, 4, b, 4, bank, wk(8))
                        link(V.tensor_tensor(G[:, ds(i * 4, 1), :], work[:, 8:9, 0:T], rs[:, :].rearrange("p (a t) -> p a t", a=1), ALU.mult))
                        softmax_front(1, T, 2, i)
                    if b == 10:
                        softmax_back(1, T, 2, i)
                    if b in (11, 13, 15):
                        n = (b - 9) // 2
                        tile_sum(p, i, 4 + n, b, 4 + n, bank, wk(8))
                        ins = V.tensor_tensor(G[:, ds(i * 4 + n, 1), :], work[:, 8:9, 0:T],
                                              rs[:, :].rearrange("p (a t) -> p a t", a=1), ALU.mult)
                        if n == 3:
                            mark(ins, S("gates_z2"), i + 1)
                        else:
                            link(ins)
                    if b == 15:
                        low_of_attention(2, i, XU)
                link.leave(p.iters)

            branches("branch2", XY)
            out_projection("out2", XU, 3, C_FFN2)
            for val in range(2):
                for edge in (0, T + 1):
                    link(V.memset(work[:, val, edge:edge + 1], 0.0))
            dve.wait_ge(rs_ready, 4)

            def ffn2(name, i):
                p, tile, c = ph[name], 0, 0
                for b, s in enumerate(FFN[name]):
                    low_part(p, i, b)
                    if b and complete(FFN[name][b - 1]):
                        u = FFN[name][b - 1]
                        z, y = work[:, u.value, 1:T + 1], wk(2 + u.value)
                        n, at = made(name, i, u.group) + u.t, ring_half(u.group, u.t)
                        ch = n + u.value * FF2
                        dve.wait_ge(S("conv_first"), n * 2 + u.value + 1)
                        link(V.scalar_tensor_tensor(y, z, convc[:, 1, ds(ch, 1)], y, ALU.mult, ALU.add))
                        ins = V.scalar_tensor_tensor(y, work[:, u.value, 2:T + 2], convc[:, 2, ds(ch, 1)], y, ALU.mult, ALU.add)
                        if u.value == 0:
                            mark(ins, S("gate_conv"), n + 1)
                        else:
                            link(ins)
                            dve.wait_ge(S("gate_silu"), n + 1)
                            mark(V.tensor_tensor(wk(5), wk(4), y, ALU.mult), S("act2_z"), n + 1)
                            dve.wait_ge(S("act2_hi"), n + 1)
                            mark(V.tensor_tensor(XY[:, at, T:2 * T], wk(5), XY[:, at, 0:T].bitcast(F32), ALU.subtract),
                                 S("act2_ready"), n + 1)
                    if complete(s):
                        z = work[:, s.value, 1:T + 1]
                        tile_sum(p, i, c, b, tile, ffn_bank(name, tile), z)
                        mark(V.tensor_tensor(z, z, rs[:, :], ALU.mult), S("conv_z"),
                             (made(name, i, s.group) + s.t) * 2 + s.value + 1)
                        c += 1
                    if s.kind == "down":
                        for k in range(2 if s.group < 0 else 1):
                            add_to_residual(p, i, b, tile + k, ffn_bank(name, tile + k), s.t + k)
                        if name == "ffn2last" and s.t >= 3:
                            copy_out(s.t - 3)
                    tile += s.half if s.kind == "up" else (2 if s.group < 0 else 1)

            def copy_out(j):
                dve.wait_ge(S("outT_full"), j + 1)
                o = Gf[:, 0:NT * D].rearrange("p (a n) -> p a n", a=NT)[:, :, j * P:(j + 1) * P]
                mark(V.tensor_copy(o, (psE, psA)[j % 2][:, 0:T].rearrange("p (a n) -> p a n", a=NT)), S("out_copied"), j + 1)

            ffn2("ffn2first", 0)
            with dve.Fori(0, ph["ffn2"].iters) as i:
                link.enter(i, 2 * (3 * KB + KD))
                ffn2("ffn2", i)
                link.leave(ph["ffn2"].iters)
            ffn2("ffn2last", 0)
            copy_out(KD - 3)
            copy_out(KD - 2)
            copy_out(KD - 1)
            dve.wait_ge(S("out_rstd"), 1)
            for c in range(2):
                part = Gf[:, c * D // 2:(c + 1) * D // 2]
                V.tensor_scalar(part, part, small[:, 6:7], None, ALU.mult).then_inc(S("out_scaled0"), 1)


PER_HEADS1 = 21
PER_HEADS2 = 15


def shape_constants():
    t = np.arange(P)
    s_, t_ = t[:, None], t[None, :]
    sums = np.zeros((9, P, P), np.float32)
    masks = np.zeros((9, P, P), np.float32)
    sums[0] = s_ > t_
    sums[8] = s_ <= t_
    masks[0] = masks[8] = np.eye(P)
    for l in range(7):
        z = 1 << l
        mid = t_ // (2 * z) * (2 * z) + z
        upper = t_ % (2 * z) >= z
        sums[l + 1] = np.where(upper, (s_ >= mid) & (s_ <= t_), (s_ > t_) & (s_ < mid))
        masks[l + 1] = (s_ // (2 * z) == t_ // (2 * z)) & (s_ % (2 * z) < z) & upper
    c = np.arange(64)
    start = np.clip(c - 8, 0, 48)
    inside = (c[None, :] >= start[:, None]) & (c[None, :] < start[:, None] + 16)
    window = np.where(inside, 0.0, MASKED).astype(np.float32)[:, ::-1]
    flat = lambda m: np.ascontiguousarray(m.transpose(1, 0, 2).reshape(P, 9 * P))
    return {"range_sums": flat(sums), "pair_masks": flat(masks), "identity": np.eye(P, dtype=np.float32),
            "window": np.concatenate([window, window])}


_INS = ["x", "w_in", "lb_logits", "hg_norm_w", "rel_bias", "w_branch_a", "w_branch_b", "w_out", "norm_mix_w",
        "norm_mlp_w", "w_up", "w_down", "norm_final_w", "norm_mix_2", "w_in_2", "gm_ln_g_2", "gm_ln_b_2",
        "gm_w_s_2", "gm_b_s_2", "na_rpb_2", "w_branch_2", "w_out_2", "norm_ffn_2", "w_up_2", "conv_k_2",
        "conv_b_2", "w_down_2", "norm_final_2"]


def kernel(**inputs):
    import concourse.bacc as bacc
    from concourse.bass_utils import run_bass_kernel_spmd

    nc = bacc.Bacc("TRN2", target_bir_lowering=False, num_devices=1, dynamic_dma_scratch_size=1024)
    arrays = {f"in_{n}": np.ascontiguousarray(inputs[n]) for n in _INS}
    arrays |= {f"in_{n}": a for n, a in shape_constants().items()}
    args = [nc.dram_tensor(n, a.shape, F32, kind="ExternalInput").ap() for n, a in arrays.items()]
    args.append(nc.dram_tensor("out_dram", (1, T, D), F32, kind="ExternalOutput").ap())
    two_blocks(nc, *args)
    r = run_bass_kernel_spmd(nc, [arrays], core_ids=[0])
    return r.results[0]["out_dram"]
```
